# Optimizing a Trainium2 kernel written in Bass

```python
import math
import jax, jax.numpy as jnp
from jax import lax
import numpy as np

D_MODEL = 1024
BATCH = 1
SEQ = 256
DEPTH = 2

N_META = 16
CHUNK = 128
D_MIX = D_MODEL
RET_HEADS = 4
RET_DK = 128
RET_DV = 128
RET_WIDTH = RET_HEADS * RET_DV
RET_THETA = 10000.0
DIFF_HEADS = 4
DIFF_D = 64
DIFF_DV = 2 * DIFF_D
DIFF_WIDTH = DIFF_HEADS * DIFF_DV
ROPE_THETA = 500000.0
ROPE_DIMS = DIFF_D // 4
D_FF = 2816
EPS = 1e-6

IN_SIZES = (
    RET_HEADS * RET_DK,
    RET_HEADS * RET_DK,
    RET_WIDTH,
    RET_WIDTH,
    DIFF_HEADS * 2 * DIFF_D,
    DIFF_HEADS * 2 * DIFF_D,
    DIFF_WIDTH,
)
D_IN = sum(IN_SIZES)


def rmsnorm(x, g):
    xf = x.astype(jnp.float32)
    y = xf * lax.rsqrt(jnp.mean(xf * xf, axis=-1, keepdims=True) + EPS)
    return (y * g.astype(jnp.float32)).astype(x.dtype)

def swiglu(x, w_gate, w_up, w_down):
    return (jax.nn.silu(x @ w_gate) * (x @ w_up)) @ w_down

def retention_rotate(x, pos):
    d = x.shape[-1]
    angle = RET_THETA ** (-jnp.linspace(0.0, 1.0, d // 2, dtype=jnp.float32))
    freqs = pos[:, None] * angle[None, :]
    cos = jnp.cos(freqs)[None, :, None, :]
    sin = jnp.sin(freqs)[None, :, None, :]
    x1, x2 = x[..., 0::2], x[..., 1::2]
    out = jnp.stack([x1 * cos - x2 * sin, x1 * sin + x2 * cos], axis=-1)
    return out.reshape(x.shape)

def partial_rope(x, pos):
    r = ROPE_DIMS
    inv = ROPE_THETA ** (-jnp.arange(0, r, 2, dtype=jnp.float32) / r)
    freqs = pos[:, None] * inv[None, :]
    emb = jnp.concatenate([freqs, freqs], axis=-1)
    cos = jnp.cos(emb)[None, :, None, None, :]
    sin = jnp.sin(emb)[None, :, None, None, :]
    xr, xp = x[..., :r], x[..., r:]
    rot = jnp.concatenate([-xr[..., r // 2:], xr[..., :r // 2]], axis=-1)
    return jnp.concatenate([xr * cos + rot * sin, xp], axis=-1)

def retention_group(q, k, v, g, gn_w):
    B, T = q.shape[0], q.shape[1]
    f32 = jnp.float32
    pos = jnp.arange(T, dtype=f32)
    q = retention_rotate(q.reshape(B, T, RET_HEADS, RET_DK).astype(f32), pos)
    k = retention_rotate(k.reshape(B, T, RET_HEADS, RET_DK).astype(f32), pos) * (RET_DK ** -0.5)
    v = v.reshape(B, T, RET_HEADS, RET_DV).astype(f32)

    n_chunks = -(-T // CHUNK)
    pad = n_chunks * CHUNK - T

    def to_chunks(t):
        t = jnp.pad(t, ((0, 0), (pad, 0), (0, 0), (0, 0)))
        return t.reshape(B, n_chunks, CHUNK, t.shape[2], t.shape[3]).transpose(0, 3, 1, 2, 4)

    qc, kc, vc = to_chunks(q), to_chunks(k), to_chunks(v)

    log_gamma = jnp.log(1.0 - 2.0 ** (-5.0 - jnp.arange(RET_HEADS, dtype=f32)))
    idx = jnp.arange(CHUNK, dtype=f32)
    rel = idx[:, None] - idx[None, :]
    decay_intra = jnp.where(rel >= 0, jnp.exp(log_gamma[:, None, None] * jnp.maximum(rel, 0.0)), 0.0)
    k_decay = jnp.exp(log_gamma[:, None] * (CHUNK - 1 - idx)[None, :])
    q_decay = jnp.exp(log_gamma[:, None] * (idx + 1.0)[None, :])
    chunk_decay = jnp.exp(log_gamma * CHUNK)

    scores = jnp.einsum('bhnid,bhnjd->bhnij', qc, kc) * decay_intra[None, :, None]
    o_intra = jnp.einsum('bhnij,bhnje->bhnie', scores, vc)

    chunk_state = jnp.einsum('bhnjd,bhnje,hj->bhnde', kc, vc, k_decay)

    def step(R, s):
        return R * chunk_decay[None, :, None, None] + s, R

    R0 = jnp.zeros((B, RET_HEADS, RET_DK, RET_DV), f32)
    _, R_prev = lax.scan(step, R0, jnp.moveaxis(chunk_state, 2, 0))
    R_prev = jnp.moveaxis(R_prev, 0, 2)
    o_cross = jnp.einsum('bhnid,bhnde,hi->bhnie', qc, R_prev, q_decay)

    o = (o_intra + o_cross).transpose(0, 2, 3, 1, 4).reshape(B, n_chunks * CHUNK, RET_HEADS, RET_DV)[:, pad:]
    mu = jnp.mean(o, axis=-1, keepdims=True)
    var = jnp.mean((o - mu) ** 2, axis=-1, keepdims=True)
    o = ((o - mu) * lax.rsqrt(var + EPS)).reshape(B, T, RET_WIDTH) * gn_w.astype(f32)
    return (jax.nn.silu(g.astype(f32)) * o).astype(g.dtype)

def diff_attention_group(q, k, v, subln_w, lq1, lk1, lq2, lk2, lambda_init):
    B, T = q.shape[0], q.shape[1]
    f32 = jnp.float32
    pos = jnp.arange(T, dtype=f32)
    q = partial_rope(q.reshape(B, T, DIFF_HEADS, 2, DIFF_D).astype(f32), pos)
    k = partial_rope(k.reshape(B, T, DIFF_HEADS, 2, DIFF_D).astype(f32), pos)
    v = v.reshape(B, T, DIFF_HEADS, DIFF_DV).astype(f32)

    lam = (jnp.exp(jnp.sum(lq1.astype(f32) * lk1.astype(f32)))
           - jnp.exp(jnp.sum(lq2.astype(f32) * lk2.astype(f32))) + lambda_init)

    n_blocks = -(-T // CHUNK)
    pad = n_blocks * CHUNK - T
    q = jnp.pad(q, ((0, 0), (pad, 0), (0, 0), (0, 0), (0, 0))).transpose(0, 2, 3, 1, 4)
    k = jnp.pad(k, ((0, 0), (pad, 0), (0, 0), (0, 0), (0, 0))).transpose(0, 2, 3, 1, 4)
    v = jnp.pad(v, ((0, 0), (pad, 0), (0, 0), (0, 0))).transpose(0, 2, 1, 3)
    scale = DIFF_D ** -0.5

    outs = []
    for nb in range(n_blocks):
        n_keys = (nb + 1) * CHUNK
        qb = q[:, :, :, nb * CHUNK:(nb + 1) * CHUNK]
        s = jnp.einsum('bhmid,bhmjd->bhmij', qb, k[:, :, :, :n_keys]) * scale
        qi = nb * CHUNK + jnp.arange(CHUNK)
        kj = jnp.arange(n_keys)
        allowed = (kj[None, :] <= qi[:, None]) & (kj[None, :] >= pad)
        p = jax.nn.softmax(jnp.where(allowed, s, -1e30), axis=-1)
        a = p[:, :, 0] - lam * p[:, :, 1]
        outs.append(jnp.einsum('bhij,bhje->bhie', a, v[:, :, :n_keys]))
    o = jnp.concatenate(outs, axis=2)[:, :, pad:].transpose(0, 2, 1, 3)
    o = o * lax.rsqrt(jnp.mean(o * o, axis=-1, keepdims=True) + EPS) * subln_w.astype(f32)
    o = o * (1.0 - lambda_init)
    return o.reshape(B, T, DIFF_WIDTH).astype(q.dtype)

def first_inputs(seed: int = 0) -> dict:
    key = jax.random.key(seed)
    ks = jax.random.split(key, 24)
    f32 = jnp.float32
    nrm = lambda k, shape, s: jax.random.normal(k, shape, f32) * s
    gain = lambda k, shape: 1.0 + 0.1 * jax.random.normal(k, shape, f32)
    return {
        "x": jax.random.normal(ks[0], (BATCH, SEQ, D_MODEL), f32),
        "meta_tokens": nrm(ks[1], (N_META, D_MODEL), 1.0),
        "ffn1_norm": gain(ks[2], (DEPTH, D_MODEL)),
        "ffn1_w_gate": nrm(ks[3], (DEPTH, D_MODEL, D_FF), D_MODEL ** -0.5),
        "ffn1_w_up": nrm(ks[4], (DEPTH, D_MODEL, D_FF), D_MODEL ** -0.5),
        "ffn1_w_down": nrm(ks[5], (DEPTH, D_FF, D_MODEL), D_FF ** -0.5),
        "mix_norm": gain(ks[6], (DEPTH, D_MODEL)),
        "w_in": nrm(ks[7], (DEPTH, D_MODEL, D_IN), D_MODEL ** -0.5),
        "ret_gn_w": gain(ks[8], (DEPTH, RET_WIDTH)),
        "diff_subln_w": gain(ks[9], (DEPTH, DIFF_DV)),
        "diff_lambda_q1": nrm(ks[10], (DEPTH, DIFF_D), 0.1),
        "diff_lambda_k1": nrm(ks[11], (DEPTH, DIFF_D), 0.1),
        "diff_lambda_q2": nrm(ks[12], (DEPTH, DIFF_D), 0.1),
        "diff_lambda_k2": nrm(ks[13], (DEPTH, DIFF_D), 0.1),
        "w_out": nrm(ks[14], (DEPTH, D_MIX, D_MODEL), D_MIX ** -0.5),
        "ffn2_norm": gain(ks[15], (DEPTH, D_MODEL)),
        "ffn2_w_gate": nrm(ks[16], (DEPTH, D_MODEL, D_FF), D_MODEL ** -0.5),
        "ffn2_w_up": nrm(ks[17], (DEPTH, D_MODEL, D_FF), D_MODEL ** -0.5),
        "ffn2_w_down": nrm(ks[18], (DEPTH, D_FF, D_MODEL), D_FF ** -0.5),
        "final_norm": gain(ks[19], (D_MODEL,)),
    }

def first_block(x, meta_tokens, ffn1_norm, ffn1_w_gate, ffn1_w_up, ffn1_w_down,
              mix_norm, w_in, ret_gn_w, diff_subln_w, diff_lambda_q1, diff_lambda_k1,
              diff_lambda_q2, diff_lambda_k2, w_out, ffn2_norm, ffn2_w_gate,
              ffn2_w_up, ffn2_w_down, final_norm):
    B = x.shape[0]
    meta = jnp.broadcast_to(meta_tokens.astype(x.dtype)[None], (B, N_META, D_MODEL))
    h = jnp.concatenate([meta, x], axis=1)
    offs = np.cumsum((0,) + IN_SIZES)

    for l in range(DEPTH):
        h = h + 0.5 * swiglu(rmsnorm(h, ffn1_norm[l]), ffn1_w_gate[l], ffn1_w_up[l], ffn1_w_down[l])

        proj = rmsnorm(h, mix_norm[l]) @ w_in[l]
        parts = [proj[..., int(offs[i]):int(offs[i + 1])] for i in range(len(IN_SIZES))]
        rq, rk, rv, rg, dq, dk, dv = parts
        lambda_init = 0.8 - 0.6 * math.exp(-0.3 * l)
        y_ret = retention_group(rq, rk, rv, rg, ret_gn_w[l])
        y_diff = diff_attention_group(dq, dk, dv, diff_subln_w[l], diff_lambda_q1[l],
                                      diff_lambda_k1[l], diff_lambda_q2[l], diff_lambda_k2[l],
                                      lambda_init)
        h = h + jnp.concatenate([y_ret, y_diff], axis=-1) @ w_out[l]

        h = h + 0.5 * swiglu(rmsnorm(h, ffn2_norm[l]), ffn2_w_gate[l], ffn2_w_up[l], ffn2_w_down[l])

    h = rmsnorm(h, final_norm)
    return h[:, N_META:]


N_MIXERS = 2
N_CONV_LAYERS = (DEPTH + 1) // 2
N_ATTN_LAYERS = DEPTH // 2
CONV_WIDTH = 3
HEAD_DIM = 64
N_HEADS = D_MODEL // HEAD_DIM
DILATION_GROUPS = ((128, 1), (512, 4), (2048, 16))
N_GROUPS = len(DILATION_GROUPS)
BLOCK = 128
N_BUCKETS = 32
MAX_EXACT = N_BUCKETS // 2
MAX_DISTANCE = 2048
RMS_EPS = 1e-6
NEG_INF = -1e30


def rmsnorm_2(x, g):
    xf = x.astype(jnp.float32)
    y = xf * lax.rsqrt(jnp.mean(xf * xf, axis=-1, keepdims=True) + RMS_EPS) * g.astype(jnp.float32)
    return y.astype(x.dtype)

def swiglu_2(h, w_in, w_out):
    gate, up = jnp.split(h @ w_in, 2, axis=-1)
    return (jax.nn.silu(gate) * up) @ w_out

def short_conv_mixer(h, w_in, w_conv, w_out):
    b_gate, c_gate, u = jnp.split(h @ w_in, 3, axis=-1)
    v = c_gate * u
    T = v.shape[1]
    vp = jnp.pad(v, ((0, 0), (CONV_WIDTH - 1, 0), (0, 0)))
    conv = sum(w_conv[lag] * vp[:, CONV_WIDTH - 1 - lag:CONV_WIDTH - 1 - lag + T]
               for lag in range(CONV_WIDTH))
    return (b_gate * conv) @ w_out

def t5_bucket(dist):
    is_small = dist < MAX_EXACT
    nf = jnp.maximum(dist, 1).astype(jnp.float32)
    large = MAX_EXACT + (jnp.log(nf / MAX_EXACT) / math.log(MAX_DISTANCE / MAX_EXACT)
                         * (N_BUCKETS - MAX_EXACT)).astype(jnp.int32)
    large = jnp.minimum(large, N_BUCKETS - 1)
    return jnp.where(is_small, dist, large)

def band_bias(rel_bias_g, dilation, n_steps):
    i = jnp.arange(BLOCK)[:, None]
    j = jnp.arange(2 * BLOCK)[None, :]
    step = BLOCK + i - j
    in_band = (step >= 0) & (step <= n_steps)
    bucket = t5_bucket(jnp.clip(step, 0, n_steps) * dilation)
    bias = rel_bias_g[bucket]
    return jnp.transpose(bias, (2, 0, 1)).astype(jnp.float32), in_band

def dilated_group(q, k, v, bias, in_band, dilation):
    B, T, H, Dh = q.shape
    span = dilation * BLOCK
    Tp = -(-T // span) * span
    L = Tp // dilation
    Lb = L // BLOCK

    def to_sub(a):
        a = jnp.pad(a, ((0, 0), (0, Tp - T), (0, 0), (0, 0))).reshape(B, L, dilation, H, Dh)
        return jnp.transpose(a, (0, 2, 1, 3, 4)).reshape(B, dilation, Lb, BLOCK, H, Dh)

    def with_prev(a):
        prev = jnp.pad(a, ((0, 0), (0, 0), (1, 0), (0, 0), (0, 0), (0, 0)))[:, :, :-1]
        return jnp.concatenate([prev, a], axis=3)

    qs = to_sub(q)
    kb = with_prev(to_sub(k))
    vb = with_prev(to_sub(v))
    logits = jnp.einsum('bsnqhd,bsnkhd->bsnhqk', qs, kb) + bias
    n_idx = jnp.arange(Lb)[:, None, None, None]
    j_idx = jnp.arange(2 * BLOCK)[None, None, None, :]
    valid = in_band[None, None] & ~((n_idx == 0) & (j_idx < BLOCK))
    logits = jnp.where(valid, logits, NEG_INF)
    m = jnp.max(logits, axis=-1, keepdims=True)
    p = jnp.exp(logits - m)
    s = jnp.sum(p, axis=-1, keepdims=True)
    o = jnp.einsum('bsnhqk,bsnkhd->bsnqhd', p, vb)
    o = o / jnp.transpose(s, (0, 1, 2, 4, 3, 5))
    lse = jnp.transpose((m + jnp.log(s))[..., 0], (0, 1, 2, 4, 3))

    def from_sub(a):
        rest = a.shape[4:]
        a = a.reshape((B, dilation, L) + rest)
        a = jnp.moveaxis(a, 1, 2).reshape((B, Tp) + rest)
        return a[:, :T]

    return from_sub(o), from_sub(lse)

def dilated_attention_mixer(h, w_qkv, q_gain, k_gain, w_out, rel_bias):
    B, T, _ = h.shape
    qkv = (h @ w_qkv).reshape(B, T, N_GROUPS, 3, N_HEADS, HEAD_DIM)
    outs, lses = [], []
    for g, (window, dilation) in enumerate(DILATION_GROUPS):
        q = rmsnorm_2(qkv[:, :, g, 0].astype(jnp.float32), q_gain[g]) * (HEAD_DIM ** -0.5)
        k = rmsnorm_2(qkv[:, :, g, 1].astype(jnp.float32), k_gain[g])
        v = qkv[:, :, g, 2].astype(jnp.float32)
        bias, in_band = band_bias(rel_bias[:, g * N_HEADS:(g + 1) * N_HEADS], dilation, window // dilation)
        o, lse = dilated_group(q, k, v, bias, in_band, dilation)
        outs.append(o)
        lses.append(lse)
    wts = jax.nn.softmax(jnp.stack(lses), axis=0)
    o = jnp.einsum('gbth,gbthd->bthd', wts, jnp.stack(outs))
    return o.reshape(B, T, N_HEADS * HEAD_DIM).astype(h.dtype) @ w_out

def second_inputs(seed: int = 0) -> dict:
    key = jax.random.key(seed)
    ks = jax.random.split(key, 16)
    f32 = jnp.float32

    def w(k, shape, fan_in):
        return jax.random.normal(k, shape, f32) * (fan_in ** -0.5)

    def gain(k, shape):
        return 1.0 + 0.05 * jax.random.normal(k, shape, f32)

    return {
        "x": jax.random.normal(ks[0], (BATCH, SEQ, D_MODEL), f32),
        "norm_ffn1": gain(ks[1], (DEPTH, D_MODEL)),
        "ffn1_w_in": w(ks[2], (DEPTH, D_MODEL, 2 * D_FF), D_MODEL),
        "ffn1_w_out": w(ks[3], (DEPTH, D_FF, D_MODEL), D_FF),
        "norm_mix": gain(ks[4], (DEPTH, D_MODEL)),
        "conv_w_in": w(ks[5], (N_CONV_LAYERS, D_MODEL, 3 * D_MODEL), D_MODEL),
        "conv_w": w(ks[6], (N_CONV_LAYERS, CONV_WIDTH, D_MODEL), CONV_WIDTH),
        "conv_w_out": w(ks[7], (N_CONV_LAYERS, D_MODEL, D_MODEL), D_MODEL),
        "attn_w_qkv": w(ks[8], (N_ATTN_LAYERS, D_MODEL, N_GROUPS * 3 * N_HEADS * HEAD_DIM), D_MODEL),
        "attn_q_gain": gain(ks[9], (N_ATTN_LAYERS, N_GROUPS, HEAD_DIM)),
        "attn_k_gain": gain(ks[10], (N_ATTN_LAYERS, N_GROUPS, HEAD_DIM)),
        "attn_w_out": w(ks[11], (N_ATTN_LAYERS, N_HEADS * HEAD_DIM, D_MODEL), N_HEADS * HEAD_DIM),
        "rel_bias": 0.5 * jax.random.normal(ks[12], (N_BUCKETS, N_GROUPS * N_HEADS), f32),
        "norm_ffn2": gain(ks[13], (DEPTH, D_MODEL)),
        "ffn2_w_in": w(ks[14], (DEPTH, D_MODEL, 2 * D_FF), D_MODEL),
        "ffn2_w_out": w(ks[15], (DEPTH, D_FF, D_MODEL), D_FF),
    }

def second_block(x, norm_ffn1, ffn1_w_in, ffn1_w_out, norm_mix, conv_w_in, conv_w, conv_w_out,
              attn_w_qkv, attn_q_gain, attn_k_gain, attn_w_out, rel_bias,
              norm_ffn2, ffn2_w_in, ffn2_w_out):
    h = x
    for i in range(DEPTH):
        h = h + 0.5 * swiglu_2(rmsnorm_2(h, norm_ffn1[i]), ffn1_w_in[i], ffn1_w_out[i])
        hn = rmsnorm_2(h, norm_mix[i])
        j = i // N_MIXERS
        if i % N_MIXERS == 0:
            mix = short_conv_mixer(hn, conv_w_in[j], conv_w[j], conv_w_out[j])
        else:
            mix = dilated_attention_mixer(hn, attn_w_qkv[j], attn_q_gain[j], attn_k_gain[j],
                                          attn_w_out[j], rel_bias)
        h = h + mix
        h = h + 0.5 * swiglu_2(rmsnorm_2(h, norm_ffn2[i]), ffn2_w_in[i], ffn2_w_out[i])
    return h


def setup_inputs(seed=0):
    out = dict(first_inputs(seed))
    for name, value in second_inputs(seed + 1).items():
        if name != "x":
            out[name + "_2"] = value
    return out


def reference(
    x, meta_tokens, ffn1_norm, ffn1_w_gate, ffn1_w_up, ffn1_w_down, mix_norm, w_in, ret_gn_w,
    diff_subln_w, diff_lambda_q1, diff_lambda_k1, diff_lambda_q2, diff_lambda_k2, w_out,
    ffn2_norm, ffn2_w_gate, ffn2_w_up, ffn2_w_down, final_norm, norm_ffn1_2, ffn1_w_in_2,
    ffn1_w_out_2, norm_mix_2, conv_w_in_2, conv_w_2, conv_w_out_2, attn_w_qkv_2, attn_q_gain_2,
    attn_k_gain_2, attn_w_out_2, rel_bias_2, norm_ffn2_2, ffn2_w_in_2, ffn2_w_out_2,
):
    x = first_block(
        x, meta_tokens, ffn1_norm, ffn1_w_gate, ffn1_w_up, ffn1_w_down, mix_norm, w_in,
        ret_gn_w, diff_subln_w, diff_lambda_q1, diff_lambda_k1, diff_lambda_q2, diff_lambda_k2,
        w_out, ffn2_norm, ffn2_w_gate, ffn2_w_up, ffn2_w_down, final_norm,
    )
    return second_block(
        x, norm_ffn1_2, ffn1_w_in_2, ffn1_w_out_2, norm_mix_2, conv_w_in_2, conv_w_2,
        conv_w_out_2, attn_w_qkv_2, attn_q_gain_2, attn_k_gain_2, attn_w_out_2, rel_bias_2,
        norm_ffn2_2, ffn2_w_in_2, ffn2_w_out_2,
    )


_drawn_inputs = setup_inputs


def setup_inputs(seed=0):
    import zlib

    import numpy as np

    out = dict(_drawn_inputs(seed))
    spreads = {}
    factors = {'attn_q_gain_2': 8.0, 'attn_k_gain_2': 8.0, 'norm_ffn2_2': 2.711}
    for name, (base, spread) in spreads.items():
        noise = np.random.default_rng([zlib.crc32(name.encode()), seed]).standard_normal(out[name].shape)
        drawn = base * np.exp(spread * noise) if base else spread * noise
        out[name] = __import__('jax').numpy.asarray(drawn.astype(out[name].dtype))
    for name, factor in factors.items():
        out[name] = (out[name] * factor).astype(out[name].dtype)
    return out
```

```python
import math
from collections import deque
from contextlib import ExitStack

import numpy as np

import concourse.bass as bass
from concourse import mybir

F32 = mybir.dt.float32
F32R = mybir.dt.float32r
ACT = mybir.ActivationFunctionType
ALU = mybir.AluOpType

P = 128
D = 1024
KC = D // P
F = 2816
FCH = F // P
META = 16
SEQ = 256
T = META + SEQ
EPS = 1e-6
NEG = -1e30
NRAW = 4
NP = 7
NH = 16
PAIR = 256

TILES = [(0, META), (META, META + P), (META + P, T)]

V_FFN1, V_MIX, V_FFN2, V_FINAL = 0, 16, 32, 48
W_FFN1, W_MIX, W_FFN2, W_CONV = 56, 72, 88, 104
V_GN, V_SUB, V_QG, V_KG = 128, 136, 138, 141
NVEC = 144


def constants():
    f = np.float32
    eye = np.eye(P, dtype=f)
    square = np.zeros((P, 5, P), f)
    square[:, 0] = eye
    square[:, 1] = eye - f(1.0 / P)
    square[:, 2] = 1.0 / P
    square[:, 3] = 1.0 / D
    square[:64, 4, :64] = 1.0 / 64
    square[64:, 4, 64:] = 1.0 / 64

    pos = np.arange(T, dtype=f)
    rot = np.zeros((P, 4, T), f)
    ang = (f(10000.0) ** (-np.linspace(0.0, 1.0, 64, dtype=f))).astype(f)
    fr = (pos[None, :] * ang[:, None]).astype(f).astype(np.float64)
    rot[0::2, 0] = rot[1::2, 0] = np.cos(fr)
    rot[0::2, 1] = -np.sin(fr)
    rot[1::2, 1] = np.sin(fr)
    inv = (f(500000.0) ** (-np.arange(0, 16, 2, dtype=f) / f(16))).astype(f)
    fr = (pos[None, :] * inv[:, None]).astype(f).astype(np.float64)
    rot[:, 2] = 1.0
    for b in (0, 64):
        rot[b:b + 8, 2] = rot[b + 8:b + 16, 2] = np.cos(fr)
        rot[b:b + 8, 3] = -np.sin(fr)
        rot[b + 8:b + 16, 3] = np.sin(fr)

    dec = np.zeros((P, 4, 384 + T), f)
    for h in range(4):
        lg = math.log(1.0 - 2.0 ** (-5.0 - h))

        def d(i, j):
            r = i - j
            return np.where(r >= 0, np.exp(lg * np.maximum(r, 0)), 0.0) * 128 ** -0.5
        a = np.arange(P)
        dec[:, h, 0:256] = d(np.arange(256)[None, :], a[:, None])
        dec[:, h, 256:384] = d(a[None, :], a[:, None])
        dec[:META, h, 384:] = d(np.arange(T)[None, :], np.arange(META)[:, None])

    mask = np.where(np.arange(T)[None, :] - (T - P) <= np.arange(P)[:, None], 0.0, NEG).astype(f)

    onehot = np.zeros((33, 3, 384), f)
    for g, (window, dil) in enumerate(((128, 1), (512, 4), (2048, 16))):
        n = window // dil
        for x in range(383):
            dist = 255 - x
            if dist >= 0 and dist % dil == 0 and dist // dil <= n:
                if dist < 16:
                    b = dist
                else:
                    v = np.log(f(dist) / f(16)) / f(math.log(2048 / 16)) * f(16)
                    b = min(16 + int(f(v)), 31)
                onehot[b, g, x] = 1.0
            else:
                onehot[32, g, x] = NEG
        onehot[32, g, 383] = NEG
    ones = np.ones((P, P), f)
    return {"c_square": square, "c_rot": rot, "c_dec": dec, "c_mask": mask,
            "c_onehot": onehot, "c_ones": ones}


class Queues:

    ENGINES = ("pe", "act", "dve", "sp", "pool")

    def __init__(self):
        self.lists = {e: [] for e in self.ENGINES}
        self.count = {}

    def op(self, e, fn, *waits):
        self.count[e] = self.count.get(e, 0) + 1
        self.lists[e].append((waits, fn, (e, 1)))
        return e, self.count[e]

    def part(self, e, fn, *waits):
        self.lists[e].append((waits, fn, None))

    def wait(self, e, *waits):
        self.lists[e].append((waits, None, None))

    def dma(self, e, sem, out, in_, *waits):
        self.count[sem] = self.count.get(sem, 0) + 16
        self.lists[e].append((waits, lambda eng: eng.dma_start(out, in_), (sem, 16)))
        return sem, self.count[sem]

    def run(self, e, eng, sems):
        reached = {}
        for waits, fn, inc in self.lists[e]:
            for w in waits:
                if w is not None and reached.get(w[0], 0) < w[1]:
                    eng.wait_ge(sems[w[0]], w[1])
                    reached[w[0]] = w[1]
            if fn is not None:
                ins = fn(eng)
                if inc is not None:
                    ins.then_inc(sems[inc[0]], inc[1])


def build(nc, A, out):
    ctx = ExitStack()
    q = Queues()
    names = [0]

    def alloc(c, shape, dt=F32):
        names[0] += 1
        return c.enter_context(nc.sbuf_tensor(f"t{names[0]}", shape, dt))

    with ctx:
        raw = alloc(ctx, [P, NRAW, 8, PAIR])
        whi = alloc(ctx, [P, NP, 8, P], F32R)
        wlo = alloc(ctx, [P, NP, 8, P], F32R)
        h = alloc(ctx, [P, KC, T])
        xh = alloc(ctx, [P, KC, T], F32R)
        xl = alloc(ctx, [P, KC, T], F32R)
        acc = alloc(ctx, [P, T])
        sq = alloc(ctx, [P, 2, T])
        rs = alloc(ctx, [P, T])
        rstd = alloc(ctx, [P, T])
        vec = alloc(ctx, [P, NVEC])
        square = alloc(ctx, [P, 5, P])
        small = alloc(ctx, [P, 32])
        IDENT, CENTRE, MEAN, MEAND, MEAN64 = (square[:, i, :] for i in range(5))
        eps = small[:, 0:1]
        lamv = small[:, 4:8].rearrange("p (l m) -> p l m", l=2)
        subw = small[:, 8:10]
        qg = small[:, 10:13]

        psp = ctx.enter_context(nc.psum_tensor("psp", [P, 4, 512], F32))
        psa = ctx.enter_context(nc.psum_tensor("psa", [P, 4, 512], F32))
        scr = nc.dram_tensor("bias_rows", [NH, 3, 384], F32, kind="Internal")
        bands = nc.dram_tensor("bias_bands", [NH * 3, P, 256], F32, kind="Internal")

        def f32(ap):
            return ap.bitcast(F32)

        units, order = [], []

        def unit(w, r0, nk, col):
            units.append((w, r0, nk, col))
            return len(units) - 1

        def pair_plan(a, b):
            order.extend([(a, 0), (b, 0), (a, 1), (b, 1)])

        def plan_ffn(gate, up, down):
            for i in range(F // PAIR):
                a = unit(gate[0], 0, 8, gate[1] + i * PAIR)
                b = unit(up[0], 0, 8, up[1] + i * PAIR)
                pair_plan(a, b)
            for i in range(D // PAIR):
                us = [unit(down, r, n, i * PAIR) for r, n in ((0, 8), (1024, 8), (2048, 6))]
                order.extend([(u, 0) for u in us] + [(u, 1) for u in us])

        def plan_cols(w, cols):
            for c in cols:
                u = unit(w, 0, 8, c)
                order.extend([(u, 0), (u, 1)])

        MIX_COLS = [PAIR * i for i in (8, 10, 12, 9, 11, 13, 0, 2, 4, 1, 3, 5, 6, 7)]
        OUT_COLS = [PAIR * i for i in range(4)]
        for l in range(2):
            plan_ffn((A["ffn1_w_gate"][l], 0), (A["ffn1_w_up"][l], 0), A["ffn1_w_down"][l])
            plan_cols(A["w_in"][l], MIX_COLS)
            plan_cols(A["w_out"][l], OUT_COLS)
            plan_ffn((A["ffn2_w_gate"][l], 0), (A["ffn2_w_up"][l], 0), A["ffn2_w_down"][l])
        for l in range(2):
            w = A["ffn1_w_in_2"][l]
            plan_ffn((w, 0), (w, F), A["ffn1_w_out_2"][l])
            if l == 0:
                w = A["conv_w_in_2"][0]
                for i in range(4):
                    a, b = unit(w, 0, 8, D + i * PAIR), unit(w, 0, 8, 2 * D + i * PAIR)
                    pair_plan(a, b)
                    plan_cols(w, [i * PAIR])
                plan_cols(A["conv_w_out_2"][0], OUT_COLS)
            else:
                plan_cols(A["attn_w_qkv_2"][0],
                          [g * 3 * D + s * D + b * PAIR for b in range(4)
                           for g, s in ((0, 0), (0, 1), (1, 0), (1, 1), (2, 0), (2, 1), (0, 2), (1, 2), (2, 2))])
                plan_cols(A["attn_w_out_2"][0], OUT_COLS)
            w = A["ffn2_w_in_2"][l]
            plan_ffn((w, 0), (w, F), A["ffn2_w_out_2"][l])

        loaded, halves = {}, {}
        highs, split, spent = [], [], []

        def load_unit(u, *waits):
            if u < len(units):
                w, r0, nk, col = units[u]
                src = w[r0:r0 + nk * P, col:col + PAIR].rearrange("(k p) n -> p k n", p=P)
                loaded[u] = q.dma("sp", f"raw{u % NRAW}", raw[:, u % NRAW, 0:nk, :], src, *waits)

        def high():
            n = len(highs)
            if n >= len(order) or n >= len(spent) + NP:
                return False
            u, half = order[n]
            nk = units[u][2]
            src = raw[:, u % NRAW, 0:nk, half * P:half * P + P]
            hi = whi[:, n % NP, 0:nk, :]
            highs.append(q.op("act", lambda e: e.activation(hi, src, ACT.Copy),
                              loaded[u], spent[n - NP] if n >= NP else None))
            return True

        def low():
            n = len(split)
            u, half = order[n]
            nk = units[u][2]
            src = raw[:, u % NRAW, 0:nk, half * P:half * P + P]
            hi, lo = whi[:, n % NP, 0:nk, :], wlo[:, n % NP, 0:nk, :]
            d = q.op("dve", lambda e: e.tensor_tensor(lo, src, f32(hi), ALU.subtract), highs[n])
            split.append(d)
            halves[u] = halves.get(u, 0) + 1
            if halves[u] == 2:
                load_unit(u + NRAW, d)

        def fill():
            got = high()
            if len(split) < len(highs) - got:
                low()

        bank_free = {}
        turn = [0]

        def next_bank():
            turn[0] += 1
            return (turn[0] - 1) % 4

        x_read = [None]

        def tiles(n, rhs, c0):
            N = T - c0
            banks = [next_bank() for _ in range(n)]
            per = -(-len(rhs) // 8)
            first = len(spent)
            while len(split) < first + n * per:
                if len(highs) == len(split):
                    high()
                low()
            for i, (k, xhi, xlo, tok) in enumerate(rhs):
                for j in range(n):
                    piece = first + j * per + k // 8
                    wh = whi[:, piece % NP, k % 8, :]
                    wl = wlo[:, piece % NP, k % 8, :]
                    o = psp[:, banks[j], 0:N]
                    start, stop = i == 0, i == len(rhs) - 1

                    def mm(e, wh=wh, wl=wl, o=o, start=start, stop=stop, xhi=xhi, xlo=xlo):
                        e.matmul(o, wh, xhi, start=start, stop=False)
                        e.matmul(o, wh, xlo, start=False, stop=False)
                        return e.matmul(o, wl, xhi, start=False, stop=stop)
                    waits = [tok, split[piece], bank_free.get(banks[j]) if start else None]
                    if stop:
                        t = q.op("pe", mm, *waits)
                        banks[j] = (banks[j], t)
                    else:
                        q.part("pe", mm, *waits)
            last = banks[-1][1]
            spent.extend([last] * (n * per))
            return banks

        xtok = [None] * KC

        def xs(c0):
            return [(k, xh[:, k, c0:T], xl[:, k, c0:T], xtok[k]) for k in range(KC)]

        acc_tok = [None]
        sq_read = [None, None]
        acc_read = [None]

        def post_chunk(m, tok, gcol, c0):
            g = vec[:, gcol + m:gcol + m + 1]
            hm = h[:, m, c0:T]
            a = q.op("act", lambda e: e.activation(xh[:, m, c0:T], hm, ACT.Copy, scale=g), tok, x_read[0])
            if m == 0:
                acc_tok[0] = q.op("act", lambda e: e.activation(acc[:, c0:T], hm, ACT.Square), acc_read[0])
            else:
                s = sq[:, m % 2, c0:T]
                b = q.op("act", lambda e: e.activation(s, hm, ACT.Square), sq_read[m % 2])
            xtok[m] = q.op("dve", lambda e: e.scalar_tensor_tensor(
                xl[:, m, c0:T], hm, g, f32(xh[:, m, c0:T]), ALU.mult, ALU.subtract), tok, a)
            if m:
                acc_tok[0] = sq_read[m % 2] = q.op("dve", lambda e: e.tensor_tensor(
                    acc[:, c0:T], acc[:, c0:T], s, ALU.add), b, acc_tok[0])

        def norm_factor(c0):
            N = T - c0
            p = q.op("pe", lambda e: e.matmul(psa[:, 0, 0:N], MEAND, acc[:, c0:T], start=True, stop=True),
                     acc_tok[0], bank_free.get(4))
            acc_read[0] = p
            a = q.op("act", lambda e: e.activation(rs[:, c0:T], psa[:, 0, 0:N], ACT.Sqrt, bias=eps), p, rs_read[0])
            bank_free[4] = a
            d = q.op("dve", lambda e: e.reciprocal(rstd[:, c0:T], rs[:, c0:T]), a)
            rs_read[0] = d
            return d

        rs_read = [None]

        def residual(c0, rhs, scale, gcol, group):
            m = 0
            while m < KC:
                n = group if m == 0 else 1
                for b, t in tiles(n, rhs, c0):
                    d = q.op("dve", lambda e, m=m, b=b: e.scalar_tensor_tensor(
                        h[:, m, c0:T], psp[:, b, 0:T - c0], scale, h[:, m, c0:T], ALU.mult, ALU.add), t)
                    bank_free[b] = d
                    if gcol is None:
                        store(m, d)
                    else:
                        post_chunk(m, d, gcol, c0)
                    for _ in range(4):
                        fill()
                    m += 1

        def store(m, d):
            done.append(q.dma("sp", "out", out[m * P:(m + 1) * P, :], h[:, m, META:T], d))

        done = []

        def phase_edge(*toks):
            for e in ("act", "dve"):
                q.wait(e, ("pe", q.count["pe"]), ("act", q.count["act"]), ("dve", q.count["dve"]), *toks)

        def silu_ffn(c0, gcol):
            N = T - c0
            region = ExitStack()
            with region:
                ah = alloc(region, [P, FCH, T], F32R)
                al = alloc(region, [P, FCH, T], F32R)
                gs = alloc(region, [P, 2, T])
                sl = alloc(region, [P, 2, T])
                us = alloc(region, [P, 2, T])
            phase_edge()
            atok = [None] * FCH
            gs_read, sl_read, us_read = [None] * 2, [None] * 2, [None] * 2

            late = []

            def lows():
                while late:
                    late.pop(0)()

            def evac(j, G, U, r):
                (bg, tg), (bu, tu) = G, U
                i = j % 2
                d1 = q.op("dve", lambda e: e.tensor_tensor(gs[:, i, 0:N], psp[:, bg, 0:N], rstd[:, c0:T], ALU.mult),
                          tg, r, gs_read[i])
                bank_free[bg] = d1
                a1 = gs_read[i] = q.op("act", lambda e: e.activation(sl[:, i, 0:N], gs[:, i, 0:N], ACT.Silu),
                                       d1, sl_read[i])
                lows()
                fill()
                d2 = q.op("dve", lambda e: e.tensor_tensor(us[:, i, 0:N], psp[:, bu, 0:N], rstd[:, c0:T], ALU.mult),
                          tu, us_read[i])
                bank_free[bu] = d2
                d3 = sl_read[i] = q.op("dve", lambda e: e.tensor_tensor(
                    us[:, i, 0:N], us[:, i, 0:N], sl[:, i, 0:N], ALU.mult), a1, d2)
                a2 = q.op("act", lambda e: e.activation(ah[:, j, 0:N], us[:, i, 0:N], ACT.Copy), d3)
                us_read[i] = a2
                fill()

                def rest():
                    atok[j] = q.op("dve", lambda e: e.tensor_tensor(
                        al[:, j, 0:N], us[:, i, 0:N], f32(ah[:, j, 0:N]), ALU.subtract), a2, d3)
                late.append(rest)

            b = tiles(4, xs(c0), c0)
            r = norm_factor(c0)
            evac(0, b[0], b[1], r)
            evac(1, b[2], b[3], r)
            for j in range(2, FCH):
                G = tiles(1, xs(c0), c0)[0]
                U = tiles(1, xs(c0), c0)[0]
                evac(j, G, U, r)
            lows()
            x_read[0] = ("pe", q.count["pe"])
            residual(c0, [(j, ah[:, j, 0:N], al[:, j, 0:N], atok[j]) for j in range(FCH)], 0.5, gcol, 1)

        def mixer(l, gcol, consts, const_tok):
            rot, dec, mask = consts
            cq = 0 if l == 0 else META
            NQ = T - cq
            qt = TILES if l == 0 else TILES[1:]
            region = ExitStack()
            with region:
                qk = alloc(region, [P, 16, T])
                rotr = alloc(region, [P, 4, T])
                m1 = alloc(region, [P, 2, T])
                sh = alloc(region, [P, 2, T])
                vt = alloc(region, [P, 8, T])
                vk = alloc(region, [P, 3, 3, P])
                sg = alloc(region, [P, 4, T])
                sm = alloc(region, [P, 2, T])
                tt = alloc(region, [P, T])
                aT = alloc(region, [P, 384])
                aT0 = alloc(region, [META, T])
                st = alloc(region, [P, 12])
                o2 = alloc(region, [P, T])
                rv = alloc(region, [P, T])
                y = alloc(region, [P, T])
                yh = alloc(region, [P, KC, T], F32R)
                yl = alloc(region, [P, KC, T], F32R)
            phase_edge()
            q.wait("dve", *const_tok)
            q.wait("pe", *const_tok)
            last = {}
            qtok, vtok, gtok, ytok = {}, {}, {}, [None] * KC
            swap2 = [i ^ 1 for i in range(32)]
            swap8 = [(i + 8) % 16 if i < 16 else i for i in range(32)]
            background = deque()
            count = [0]

            def step():
                while background:
                    try:
                        next(background[0])
                        return
                    except StopIteration:
                        background.popleft()

            def rotate(i, b, t, kind, c0):
                s = count[0] % 2
                count[0] += 1
                n = T - c0
                src = psp[:, b, 0:n]
                cos, sin = rotr[:, 2 * kind, c0:T], rotr[:, 2 * kind + 1, c0:T]
                d1 = q.op("dve", lambda e: e.stream_shuffle(sh[:, s, 0:n], src, swap8 if kind else swap2), t)
                d2 = q.op("dve", lambda e: e.tensor_tensor(m1[:, s, 0:n], src, cos, ALU.mult), rtok[1])
                bank_free[b] = d2
                d3 = q.op("dve", lambda e: e.tensor_tensor(sh[:, s, 0:n], sh[:, s, 0:n], sin, ALU.mult), d1)
                fill()
                qtok[i] = q.op("dve", lambda e: e.tensor_tensor(qk[:, i, c0:T], m1[:, s, 0:n], sh[:, s, 0:n], ALU.add), d3)

            def values(i, b, t):
                d = q.op("dve", lambda e: e.tensor_tensor(vt[:, i, :], psp[:, b, 0:T], rstd[:, :], ALU.mult),
                         t, last.get(("vt", i)))
                bank_free[b] = d
                vtok[i] = d

            def gate(i, b, t):
                d = q.op("dve", lambda e: e.tensor_tensor(sg[:, i, cq:T], psp[:, b, 0:NQ], rstd[:, cq:T], ALU.mult), t)
                bank_free[b] = d
                gtok[i] = q.op("act", lambda e: e.activation(sg[:, i, cq:T], sg[:, i, cq:T], ACT.Silu), d)

            def token_major(i, basis):
                s = i % 3

                def mm(e):
                    for k, (a, z) in enumerate(TILES):
                        x = e.matmul(psa[0:z - a, 3, k * P:(k + 1) * P], vt[:, i, a:z], basis,
                                     start=True, stop=True)
                    return x
                p = last["vt", i] = q.op("pe", mm, vtok[i], bank_free.get(7))
                q.op("act", lambda e: e.activation(vk[:, s, 1:3, :], psa[:, 3, P:3 * P].rearrange(
                    "p (k n) -> p k n", k=2), ACT.Copy), p, last.get(("vk", s)))
                a = q.op("act", lambda e: e.activation(vk[0:META, s, 0, :], psa[0:META, 3, 0:P], ACT.Copy))
                bank_free[7] = a
                return s, a

            def mix_values(i, s, w12, w0, bank, *toks):
                def mm(e):
                    o = psa[:, bank - 4, :]
                    e.matmul(o[:, 0:NQ], vk[0:META, s, 0, :], w0[:, cq:T], start=True, stop=False)
                    a = META - cq
                    e.matmul(o[:, a:NQ], vk[:, s, 1, :], w12[:, 0:256], start=False, stop=False)
                    return e.matmul(o[:, a + P:NQ], vk[:, s, 2, :], w12[:, 256:384], start=False, stop=True)
                p = last["vk", s] = q.op("pe", mm, *toks, bank_free.get(bank))
                return p

            def normalise(bank, p, w, other):
                o = psa[:, bank - 4, 0:NQ]
                a = q.op("act", lambda e: e.activation(o2[:, 0:NQ], o, ACT.Square), p, last.get("o2"))
                yield
                m = last["o2"] = q.op("pe", lambda e: e.matmul(psa[:, other - 4, 0:NQ], MEAN, o2[:, 0:NQ],
                                                                start=True, stop=True), a, bank_free.get(other))
                a = q.op("act", lambda e: e.activation(rv[:, 0:NQ], psa[:, other - 4, 0:NQ], ACT.Sqrt, bias=eps),
                         m, last.get("rv"))
                bank_free[other] = a
                d = q.op("dve", lambda e: e.reciprocal(rv[:, 0:NQ], rv[:, 0:NQ]), a)
                d = q.op("dve", lambda e: e.scalar_tensor_tensor(y[:, 0:NQ], o, w, rv[:, 0:NQ], ALU.mult, ALU.mult),
                         d, last.get("y"))
                last["rv"] = d
                bank_free[bank] = d
                last["made"] = d

            def emit_y(c, d):
                a = q.op("act", lambda e: e.activation(yh[:, c, cq:T], y[:, 0:NQ], ACT.Copy), d)
                last["y"] = a
                ytok[c] = q.op("dve", lambda e: e.tensor_tensor(yl[:, c, cq:T], y[:, 0:NQ],
                                                                f32(yh[:, c, cq:T]), ALU.subtract), a, d)

            def diff_head(i):
                s, vdone = token_major(i, IDENT)
                qi, ki = 8 + i, 12 + i
                yield
                for n, (a, z) in enumerate(qt):
                    r, N = z - a, z

                    def scores(e, a=a, z=z, r=r, N=N):
                        for m in range(2):
                            x = e.matmul(psa[0:r, m, 0:N], qk[64 * m:64 * m + 64, qi, a:z],
                                         qk[64 * m:64 * m + 64, ki, 0:N], start=True, stop=True)
                        return x
                    p = q.op("pe", scores, qtok[qi], qtok[ki], bank_free.get(4), bank_free.get(5))
                    for m in range(2):
                        d = q.op("dve", lambda e, m=m, r=r, N=N: e.tensor_tensor_reduce(
                            out=sm[0:r, m, 0:N], in0=psa[0:r, m, 0:N], in1=mask[0:r, T - N:T] if r == P
                            else mask[0:r, T - P:T - P + N],
                            scale=1.0, scalar=-3.0e38, op0=ALU.add, op1=ALU.max,
                            accum_out=st[0:r, m:m + 1]), p, last.get("tt"))
                    bank_free[4] = bank_free[5] = d
                    d = q.op("dve", lambda e, r=r: e.tensor_scalar(st[0:r, 2:4], st[0:r, 0:2], -0.125, None, ALU.mult), d)
                    for m in range(2):
                        x = q.op("act", lambda e, m=m, r=r, N=N: e.activation(
                            sm[0:r, m, 0:N], sm[0:r, m, 0:N], ACT.Exp, bias=st[0:r, 2 + m:3 + m], scale=0.125,
                            accum_out=st[0:r, 4 + m:5 + m]), d)
                    fill()
                    d = q.op("dve", lambda e, r=r: e.reciprocal(st[0:r, 6:8], st[0:r, 4:6]), x)
                    d = q.op("dve", lambda e, r=r: e.tensor_tensor(st[0:r, 8:10], st[0:r, 6:8], lamv[0:r, l, :], ALU.mult), d)
                    d = q.op("dve", lambda e, r=r, N=N: e.tensor_scalar(sm[0:r, 1, 0:N], sm[0:r, 1, 0:N], st[0:r, 9:10],
                                                                        None, ALU.mult), d)
                    d = q.op("dve", lambda e, r=r, N=N: e.scalar_tensor_tensor(
                        tt[0:r, 0:N], sm[0:r, 0, 0:N], st[0:r, 8:9], sm[0:r, 1, 0:N], ALU.mult, ALU.add), d)
                    yield

                    def turn_over(e, a=a, z=z, r=r):
                        x = e.matmul(psa[0:META, 3, a:z], tt[0:r, 0:META], IDENT[0:r, 0:r], start=True, stop=True)
                        if a >= META:
                            x = e.transpose(psa[:, 2, a - META:z - META], tt[0:r, META:META + P], IDENT)
                        if a >= META + P:
                            x = e.transpose(psa[:, 2, 256:384], tt[0:r, META + P:T], IDENT)
                        return x
                    first = n == 0
                    last["tt"] = q.op("pe", turn_over, d, bank_free.get(6) if first else None,
                                      bank_free.get(7) if first else None)
                p = last["tt"]
                x0 = q.op("act", lambda e: e.activation(aT[:, :], psa[:, 2, 0:384], ACT.Copy), p, last.get("aT"))
                x1 = q.op("act", lambda e: e.activation(aT0[:, cq:T], psa[0:META, 3, cq:T], ACT.Copy))
                bank_free[6] = x0
                bank_free[7] = x1
                yield
                p = last["aT"] = mix_values(i, s, aT, aT0, 6, x1)
                yield from normalise(6, p, subw[:, l:l + 1], 7)
                emit_y(4 + i, last["made"])
                yield

            def ret_head(i):
                s, vdone = token_major(4 + i, CENTRE)
                qi, ki = i, 4 + i
                yield

                def scores(e):
                    e.matmul(psa[0:META, 1, 0:NQ], qk[:, ki, 0:META], qk[:, qi, cq:T], start=True, stop=True)
                    e.matmul(psa[:, 0, 0:256], qk[:, ki, META:META + P], qk[:, qi, META:T], start=True, stop=True)
                    return e.matmul(psa[:, 0, 256:384], qk[:, ki, META + P:T], qk[:, qi, META + P:T],
                                    start=True, stop=True)
                p = q.op("pe", scores, qtok[qi], qtok[ki], bank_free.get(4), bank_free.get(5))
                q.op("dve", lambda e: e.tensor_tensor(aT0[:, cq:T], psa[0:META, 1, 0:NQ],
                                                      dec[0:META, i, 384 + cq:384 + T], ALU.mult), p, last.get("aT"))
                d = q.op("dve", lambda e: e.tensor_tensor(aT[:, :], psa[:, 0, 0:384], dec[:, i, 0:384], ALU.mult))
                bank_free[4] = bank_free[5] = d
                yield
                p = last["aT"] = mix_values(4 + i, s, aT, aT0, 6, d, vdone)
                yield from normalise(6, p, vec[:, V_GN + 4 * l + i:V_GN + 4 * l + i + 1], 5)
                while i not in gtok:
                    yield
                d = q.op("dve", lambda e: e.tensor_tensor(y[:, 0:NQ], y[:, 0:NQ], sg[:, i, cq:T], ALU.mult),
                         gtok[i], last["made"])
                emit_y(i, d)
                yield

            kinds = [("dq", 0), ("dk", 0), ("dv", 0), ("dq", 2), ("dk", 2), ("dv", 2), ("rq", 0), ("rk", 0),
                     ("rv", 0), ("rq", 2), ("rk", 2), ("rv", 2), ("rg", 0), ("rg", 2)]
            rtok = [None, None]

            def evac(kind, i, b, t):
                if kind == "dq":
                    rotate(8 + i, b, t, 1, cq)
                elif kind == "dk":
                    rotate(12 + i, b, t, 1, 0)
                elif kind == "rq":
                    rotate(i, b, t, 0, cq)
                elif kind == "rk":
                    rotate(4 + i, b, t, 0, 0)
                elif kind == "dv":
                    values(i, b, t)
                    background.append(diff_head(i))
                elif kind == "rv":
                    values(4 + i, b, t)
                    background.append(ret_head(i))
                else:
                    gate(i, b, t)

            start = {"dq": cq, "rq": cq, "rg": cq}
            assert cq == 0 or start["dq"] == META
            pend = tiles_mixed = None
            b = tiles(2, xs(cq), cq)
            b += tiles(2, xs(0), 0)
            r = norm_factor(0)
            rtok[0] = r
            for j in range(4):
                rtok[1] = q.op("dve", lambda e, j=j: e.tensor_tensor(rotr[:, j, :], rot[:, j, :], rstd[:, :], ALU.mult),
                               r if j == 0 else None)
            for j, (bk, t) in enumerate(b):
                evac(kinds[j // 2][0], kinds[j // 2][1] + j % 2, bk, t)
            for kind, i in kinds[2:]:
                for j in range(2):
                    c0 = start.get(kind, 0)
                    bk, t = tiles(1, xs(c0), c0)[0]
                    step()
                    evac(kind, i + j, bk, t)
                    fill()
            while background:
                step()
            x_read[0] = ("pe", q.count["pe"])
            ks = [4, 5, 6, 7, 0, 1, 2, 3]
            residual(cq, [(k, yh[:, k, cq:T], yl[:, k, cq:T], ytok[k]) for k in ks], 1.0, gcol, 4)

        def conv_mixer(gcol):
            c0 = META
            region = ExitStack()
            with region:
                cs = alloc(region, [P, 2, SEQ])
                us = alloc(region, [P, 2, SEQ])
                vp = alloc(region, [P, 2, SEQ + 2])
                cv = alloc(region, [P, 4, SEQ])
                y = alloc(region, [P, 2, SEQ])
                yh = alloc(region, [P, KC, SEQ], F32R)
                yl = alloc(region, [P, KC, SEQ], F32R)
            phase_edge()
            z = q.op("dve", lambda e: e.memset(vp[:, :, 0:2], 0.0))
            ytok, cvtok, yread = [None] * KC, [None] * KC, [None] * 2
            r = [None]

            def conv(j, C, U):
                i = j % 2
                d1 = q.op("dve", lambda e: e.tensor_tensor(cs[:, i, :], psp[:, C[0], 0:SEQ], rstd[:, c0:T], ALU.mult),
                          C[1], r[0])
                bank_free[C[0]] = d1
                d2 = q.op("dve", lambda e: e.tensor_tensor(us[:, i, :], psp[:, U[0], 0:SEQ], rstd[:, c0:T], ALU.mult), U[1])
                bank_free[U[0]] = d2
                d3 = q.op("dve", lambda e: e.tensor_tensor(vp[:, i, 2:], cs[:, i, :], us[:, i, :], ALU.mult), d2)
                o = cv[:, j % 4, :]
                d = q.op("dve", lambda e: e.tensor_scalar(o, vp[:, i, 2:], vec[:, W_CONV + j:W_CONV + j + 1],
                                                          None, ALU.mult), d3, z)
                fill()
                for lag in (1, 2):
                    w = vec[:, W_CONV + 8 * lag + j:W_CONV + 8 * lag + j + 1]
                    d = q.op("dve", lambda e, lag=lag, w=w: e.scalar_tensor_tensor(
                        o, vp[:, i, 2 - lag:2 - lag + SEQ], w, o, ALU.mult, ALU.add), d)
                cvtok[j] = d

            def gate(j, B):
                i = j % 2
                d = q.op("dve", lambda e: e.tensor_tensor(y[:, i, :], psp[:, B[0], 0:SEQ], rstd[:, c0:T], ALU.mult),
                         B[1], yread[i])
                bank_free[B[0]] = d
                d = q.op("dve", lambda e: e.tensor_tensor(y[:, i, :], y[:, i, :], cv[:, j % 4, :], ALU.mult), d, cvtok[j])
                a = yread[i] = q.op("act", lambda e: e.activation(yh[:, j, :], y[:, i, :], ACT.Copy), d)
                fill()
                ytok[j] = q.op("dve", lambda e: e.tensor_tensor(yl[:, j, :], y[:, i, :], f32(yh[:, j, :]), ALU.subtract), a)

            for i in range(4):
                if i == 0:
                    b = tiles(4, xs(c0), c0)
                    r[0] = norm_factor(c0)
                    conv(0, b[0], b[1])
                    conv(1, b[2], b[3])
                else:
                    for j in range(2):
                        C = tiles(1, xs(c0), c0)[0]
                        U = tiles(1, xs(c0), c0)[0]
                        conv(2 * i + j, C, U)
                for j in range(2):
                    gate(2 * i + j, tiles(1, xs(c0), c0)[0])
            x_read[0] = ("pe", q.count["pe"])
            residual(c0, [(k, yh[:, k, :], yl[:, k, :], ytok[k]) for k in range(KC)], 1.0, gcol, 4)

        def dilated_mixer(gcol, band_tok):
            c0 = META
            region = ExitStack()
            with region:
                qk = alloc(region, [P, 2, 2, 3, 2, SEQ])
                vt = alloc(region, [P, 2, SEQ])
                vk = alloc(region, [P, 2, 2, 3, SEQ])
                sqb = alloc(region, [P, 2, SEQ])
                rq = alloc(region, [P, 512])
                bias = alloc(region, [P, 2, 3, 256])
                p1 = alloc(region, [P, 3, 256])
                p0 = alloc(region, [P, 3, P])
                pT = alloc(region, [P, 3, 384])
                st = alloc(region, [P, 8])
                yh = alloc(region, [P, KC, SEQ], F32R)
                yl = alloc(region, [P, KC, SEQ], F32R)
            phase_edge()
            q.wait("pool", ("pe", q.count["pe"]), ("act", q.count["act"]), ("dve", q.count["dve"]))
            last, ytok = {}, [None] * KC
            qktok, vktok = {}, {}
            s1 = psa[:, 0:2, :].rearrange("p b n -> p (b n)")[:, 0:768].rearrange("p (g n) -> p g n", g=3)
            s0 = psa[:, 2, 0:384].rearrange("p (g n) -> p g n", g=3)
            background, after = deque(), deque()
            bias_tok = {}

            def load_bias(n, *waits):
                if n < NH:
                    src = bands.ap()[3 * n:3 * n + 3].rearrange("g i x -> i g x")
                    bias_tok[n] = q.dma("pool", f"bias{n % 2}", bias[:, n % 2, :, :], src, band_tok, *waits)

            load_bias(0)
            load_bias(1)

            def step():
                while background:
                    try:
                        next(background[0])
                        return
                    except StopIteration:
                        background.popleft()

            def head(n):
                b, pair, r = n // 4, n // 2 % 2, n % 2
                rows = slice(64 * r, 64 * r + 64)
                B = bias[:, n % 2, :, :]

                def Q(g, s):
                    return qk[rows, b % 2, pair, g, s, :]

                def scores(e):
                    for g in range(3):
                        e.matmul(s1[:, g, :], Q(g, 0)[:, P:SEQ], Q(g, 1), start=True, stop=True)
                    for g in range(3):
                        x = e.matmul(s0[:, g, :], Q(g, 0)[:, 0:P], Q(g, 1)[:, 0:P], start=True, stop=True)
                    return x
                p = q.op("pe", scores, qktok[b, pair], bank_free.get(4), bank_free.get(5), bank_free.get(6))
                last["qk", b % 2] = p
                d1 = q.op("dve", lambda e: e.tensor_tensor_reduce(
                    out=p1[:, :, :], in0=s1, in1=B, scale=1.0, scalar=-3.0e38, op0=ALU.add, op1=ALU.max,
                    accum_out=st[:, 0:1]), p, bias_tok[n], last.get("p"))
                d0 = q.op("dve", lambda e: e.tensor_tensor_reduce(
                    out=p0[:, :, :], in0=s0, in1=B[:, :, P:256], scale=1.0, scalar=-3.0e38, op0=ALU.add, op1=ALU.max,
                    accum_out=st[:, 1:2]))
                bank_free[4] = bank_free[5] = d1
                bank_free[6] = d0
                load_bias(n + 2, d0)
                d = q.op("dve", lambda e: e.tensor_scalar(st[:, 2:4], st[:, 0:2], -1.0, None, ALU.mult), d0)
                q.op("act", lambda e: e.activation(p1[:, :, :], p1[:, :, :], ACT.Exp, bias=st[:, 2:3],
                                                   accum_out=st[:, 4:5]), d)
                a = q.op("act", lambda e: e.activation(p0[:, :, :], p0[:, :, :], ACT.Exp, bias=st[:, 3:4],
                                                       accum_out=st[:, 5:6]))
                fill()
                d = q.op("dve", lambda e: e.reciprocal(st[:, 6:8], st[:, 4:6]), a)
                q.op("dve", lambda e: e.tensor_scalar(p1[:, :, :], p1[:, :, :], st[:, 6:7], None, ALU.mult), d)
                d = q.op("dve", lambda e: e.tensor_scalar(p0[:, :, :], p0[:, :, :], st[:, 7:8], None, ALU.mult))
                yield

                def turn_over(e):
                    for g in range(3):
                        e.transpose(psa[:, 3, g * P:(g + 1) * P], p0[:, g, :], IDENT)
                    for g in range(3):
                        for j in range(2):
                            x = e.transpose(s1[:, g, j * P:(j + 1) * P], p1[:, g, j * P:(j + 1) * P], IDENT)
                    return x
                p = last["p"] = q.op("pe", turn_over, d, bank_free.get(7), bank_free[4])
                a0 = q.op("act", lambda e: e.activation(pT[:, :, 0:P], psa[:, 3, 0:384].rearrange(
                    "p (g n) -> p g n", g=3), ACT.Copy), p, last.get("pT"))
                bank_free[7] = a0
                a1 = q.op("act", lambda e: e.activation(pT[:, :, P:384], s1, ACT.Copy))
                bank_free[4] = bank_free[5] = a1
                yield

                def mix(e):
                    o = psa[rows, 2, 0:SEQ]
                    c = slice(64 * (n % 4), 64 * (n % 4) + 64)
                    for g in range(3):
                        e.matmul(o, vk[:, b % 2, 0, g, c], pT[:, g, 0:256], start=g == 0, stop=False)
                    for g in range(3):
                        x = e.matmul(o[:, P:SEQ], vk[:, b % 2, 1, g, c], pT[:, g, 256:384], start=False, stop=g == 2)
                    return x
                p = last["pT"] = last["vk", b % 2] = q.op("pe", mix, a1, vktok[b], bank_free[6])
                ch = n // 2
                a = q.op("act", lambda e: e.activation(yh[rows, ch, :], psa[rows, 2, 0:SEQ], ACT.Copy), p)
                d = q.op("dve", lambda e: e.tensor_tensor(yl[rows, ch, :], psa[rows, 2, 0:SEQ],
                                                          f32(yh[rows, ch, :]), ALU.subtract), a)
                bank_free[6] = d
                ytok[ch] = d
                yield

            def qk_norm(b, g, s):
                toks = last["sq"]

                def mm(e):
                    for pair in range(2):
                        x = e.matmul(psa[:, 3, pair * SEQ:(pair + 1) * SEQ], MEAN64, sqb[:, pair, :],
                                     start=True, stop=True)
                    return x
                p = last["sqr"] = q.op("pe", mm, toks, bank_free.get(7))
                a = q.op("act", lambda e: e.activation(rq[:, :], psa[:, 3, :], ACT.Sqrt, bias=eps), p, last.get("rq"))
                bank_free[7] = a
                d = q.op("dve", lambda e: e.reciprocal(rq[:, :], rq[:, :]), a)
                w = qg[:, g:g + 1] if s == 0 else vec[:, V_KG + g:V_KG + g + 1]
                for pair in range(2):
                    o = qk[:, b % 2, pair, g, s, :]
                    qktok[b, pair] = q.op("dve", lambda e, o=o, pair=pair: e.scalar_tensor_tensor(
                        o, o, w, rq[:, pair * SEQ:(pair + 1) * SEQ], ALU.mult, ALU.mult), d)
                last["rq"] = qktok[b, 1]

            def v_turn(b, g, pair, d):
                def mm(e):
                    for j in range(2):
                        x = e.transpose(psa[:, 3, j * P:(j + 1) * P], vt[:, pair, j * P:(j + 1) * P], IDENT)
                    return x
                p = last["vt", pair] = q.op("pe", mm, d, bank_free.get(7))
                a = q.op("act", lambda e: e.activation(
                    vk[:, b % 2, :, g, pair * P:(pair + 1) * P],
                    psa[:, 3, 0:256].rearrange("p (j n) -> p j n", j=2), ACT.Copy), p, last.get(("vk", b % 2)))
                bank_free[7] = a
                vktok[b] = a

            r = [None]

            def evac(b, g, s, pair, bk, t):
                src = psp[:, bk, 0:SEQ]
                if s < 2:
                    o = qk[:, b % 2, pair, g, s, :]
                    d = q.op("dve", lambda e: e.tensor_tensor(o, src, rstd[:, c0:T], ALU.mult),
                             t, r[0], last.get(("qk", b % 2)))
                    bank_free[bk] = d
                    last["sq"] = q.op("act", lambda e: e.activation(sqb[:, pair, :], o, ACT.Square), d, last.get("sqr"))
                    if pair:
                        after.append(lambda: qk_norm(b, g, s))
                else:
                    d = q.op("dve", lambda e: e.tensor_tensor(vt[:, pair, :], src, rstd[:, c0:T], ALU.mult),
                             t, last.get(("vt", pair)))
                    bank_free[bk] = d
                    after.append(lambda: v_turn(b, g, pair, d))

            seq = [(g, s) for g in range(3) for s in range(2)] + [(g, 2) for g in range(3)]
            for b in range(4):
                for n, (g, s) in enumerate(seq):
                    if b == 0 and n == 0:
                        banks = tiles(4, xs(c0), c0)
                        r[0] = norm_factor(c0)
                        for i, (bk, t) in enumerate(banks):
                            if i == 2:
                                after.popleft()()
                            evac(0, 0, i // 2, i % 2, bk, t)
                        continue
                    if b == 0 and n == 1:
                        continue
                    for pair in range(2):
                        bk, t = tiles(1, xs(c0), c0)[0]
                        while after:
                            after.popleft()()
                        if n in (2, 3, 4, 6, 7, 8):
                            step()
                        fill()
                        evac(b, g, s, pair, bk, t)
                        fill()
                while background:
                    step()
                while after:
                    after.popleft()()
                background.extend(head(4 * b + i) for i in range(4))
            while background:
                step()
            x_read[0] = ("pe", q.count["pe"])
            residual(c0, [(k, yh[:, k, :], yl[:, k, :], ytok[k]) for k in range(KC)], 1.0, gcol, 4)

        htok = q.dma("sp", "h", h[:, :, :], A["hT"].rearrange("(k p) t -> p k t", p=P))
        vectok = q.dma("act", "vec", vec[:, :], A["vec"])
        sqtok = q.dma("pool", "sqc", square[:, :, :], A["c_square"])
        for u in range(NRAW):
            load_unit(u)
        e0 = q.op("dve", lambda e: e.memset(small[:, :], 0.0))
        e0 = q.op("dve", lambda e: e.memset(eps, EPS), e0)
        e0 = q.op("dve", lambda e: e.memset(lamv[:, :, 0:1], 1.0), e0)
        q.wait("act", vectok, e0)
        q.wait("dve", vectok)
        q.wait("pe", sqtok)

        block1 = ExitStack()
        with block1:
            rot = alloc(block1, [P, 4, T])
            dec = alloc(block1, [P, 4, 384 + T])
            mask = alloc(block1, [P, T])
            start = ExitStack()
            with start:
                oh = alloc(start, [33, 3, 384])
                rb = alloc(start, [33, 48])
                eb = alloc(start, [NH, 3, 384])
                lam = alloc(start, [64, 16])
                ones = alloc(start, [P, P])
            inits = [q.dma("pool", "init", oh[:, :, :], A["c_onehot"]),
                     q.dma("pool", "init", rb[0:32, :], A["rel_bias_2"]),
                     q.dma("pool", "init", rb[32:33, :], A["c_ones"][0:1, 0:48]),
                     q.dma("pool", "init", lam[:, 0:8], A["lam"]),
                     q.dma("pool", "init", ones[:, :], A["c_ones"])]
            itok = inits[-1]
            consts = [q.dma("pool", "const", rot[:, :, :], A["c_rot"]),
                      q.dma("pool", "const", dec[:, :, :], A["c_dec"]),
                      q.dma("pool", "const", mask[:, :], A["c_mask"])]
            for m in range(KC):
                post_chunk(m, htok, V_FFN1, 0)
            d = q.op("dve", lambda e: e.tensor_tensor(lam[:, 8:12], lam[:, 0:4], lam[:, 4:8], ALU.mult), itok)

            def start_mm(e):
                e.matmul(psa[:, 3, 0:4], ones[0:64, :], lam[:, 8:12], start=True, stop=True)
                for g in range(3):
                    x = e.matmul(psa[0:NH, g, 0:384], rb[:, 16 * g:16 * g + 16], oh[:, g, :], start=True, stop=True)
                return x
            p = q.op("pe", start_mm, d, itok)
            for g in range(3):
                dd = q.op("dve", lambda e, g=g: e.tensor_copy(eb[:, g, :], psa[0:NH, g, 0:384]), p)
            bank_free[4] = bank_free[5] = bank_free[6] = dd
            scr_tok = q.dma("pool", "scr", scr.ap(), eb[:, :, :], dd)
            band_tok = q.dma("pool", "bands", bands.ap(),
                             bass.AP(scr, 127, [[384, NH * 3], [-1, P], [1, 256]]), scr_tok)
            a = q.op("act", lambda e: e.activation(small[:, 16:20], psa[:, 3, 0:4], ACT.Exp), p)
            bank_free[7] = a
            for l in range(2):
                li = 0.8 - 0.6 * math.exp(-0.3 * l)
                d = q.op("dve", lambda e, l=l: e.tensor_tensor(
                    small[:, 20 + l:21 + l], small[:, 18 + l:19 + l], small[:, 16 + l:17 + l], ALU.subtract), a)
                d = q.op("dve", lambda e, l=l, li=li: e.tensor_scalar(
                    lamv[:, l, 1:2], small[:, 20 + l:21 + l], -li, None, ALU.add), d)
                d = q.op("dve", lambda e, l=l, li=li: e.tensor_scalar(
                    subw[:, l:l + 1], vec[:, V_SUB + l:V_SUB + l + 1], 1.0 - li, None, ALU.mult))
            d = q.op("dve", lambda e: e.tensor_scalar(qg, vec[:, V_QG:V_QG + 3], 0.125, None, ALU.mult))
            q.wait("act", scr_tok)
            q.wait("dve", scr_tok)

            silu_ffn(0, V_MIX)
            mixer(0, V_FFN2, (rot, dec, mask), [consts[-1]])
            silu_ffn(0, V_FFN1 + 8)
            silu_ffn(0, V_MIX + 8)
            mixer(1, V_FFN2 + 8, (rot, dec, mask), [])
            silu_ffn(META, V_FINAL)
        r = norm_factor(META)
        for m in range(KC):
            g = vec[:, V_FINAL + m:V_FINAL + m + 1]
            d = q.op("dve", lambda e, m=m, g=g: e.scalar_tensor_tensor(
                h[:, m, META:T], h[:, m, META:T], g, rstd[:, META:T], ALU.mult, ALU.mult), r)
            post_chunk(m, d, W_FFN1, META)
        silu_ffn(META, W_MIX)
        conv_mixer(W_FFN2)
        silu_ffn(META, W_FFN1 + 8)
        silu_ffn(META, W_MIX + 8)
        dilated_mixer(W_FFN2 + 8, band_tok)
        silu_ffn(META, None)
        q.wait("sp", done[-1])
        assert len(spent) == len(order) and len(split) == len(order)

        sems = {s: ctx.enter_context(nc.semaphore(f"s_{s}")) for s in q.count}
        block = ctx.enter_context(nc.Block())

        @block.sync
        def _(eng):
            q.run("sp", eng, sems)

        @block.gpsimd
        def _(eng):
            q.run("pool", eng, sems)

        @block.scalar
        def _(eng):
            q.run("act", eng, sems)

        @block.vector
        def _(eng):
            q.run("dve", eng, sems)

        @block.tensor
        def _(eng):
            q.run("pe", eng, sems)


WEIGHTS = ["ffn1_w_gate", "ffn1_w_up", "ffn1_w_down", "w_in", "w_out", "ffn2_w_gate", "ffn2_w_up", "ffn2_w_down",
           "ffn1_w_in_2", "ffn1_w_out_2", "conv_w_in_2", "conv_w_out_2", "attn_w_qkv_2", "attn_w_out_2",
           "rel_bias_2", "ffn2_w_in_2", "ffn2_w_out_2"]


def kernel(**inputs):
    import concourse.bacc as bacc
    from concourse.bass_utils import run_bass_kernel_spmd

    a = {k: np.ascontiguousarray(v) for k, v in inputs.items()}

    def cols(v):
        return v.reshape(-1, KC, P).transpose(2, 0, 1).reshape(P, -1)

    vec = np.concatenate(
        [cols(a[n]) for n in ("ffn1_norm", "mix_norm", "ffn2_norm", "final_norm", "norm_ffn1_2", "norm_mix_2",
                              "norm_ffn2_2", "conv_w_2")]
        + [a["ret_gn_w"].reshape(8, P).T, a["diff_subln_w"].T]
        + [np.concatenate([a[n][0].T, a[n][0].T], axis=0) for n in ("attn_q_gain_2", "attn_k_gain_2")], axis=1)
    lam = np.concatenate([a[n] for n in ("diff_lambda_q1", "diff_lambda_q2", "diff_lambda_k1", "diff_lambda_k2")]).T
    arrays = {n: a[n] for n in WEIGHTS}
    arrays["hT"] = np.ascontiguousarray(np.concatenate([a["meta_tokens"], a["x"][0]]).T)
    arrays["vec"] = np.ascontiguousarray(vec)
    arrays["lam"] = np.ascontiguousarray(lam)
    arrays.update(constants())

    nc = bacc.Bacc("TRN2", target_bir_lowering=False, num_devices=1)
    aps = {n: nc.dram_tensor(n, v.shape, mybir.dt.from_np(v.dtype), kind="ExternalInput").ap()
           for n, v in arrays.items()}
    out = nc.dram_tensor("outT", (D, SEQ), F32, kind="ExternalOutput").ap()
    build(nc, aps, out)
    r = run_bass_kernel_spmd(nc, [arrays], core_ids=[0])
    return np.ascontiguousarray(r.results[0]["outT"].T).reshape(1, SEQ, D)
```

```python
import math
from collections import deque
from contextlib import ExitStack

import numpy as np

import concourse.bass as bass
from concourse import mybir

F32 = mybir.dt.float32
F32R = mybir.dt.float32r
ACT = mybir.ActivationFunctionType
ALU = mybir.AluOpType

P = 128
D = 1024
KC = D // P
F = 2816
FCH = F // P
META = 16
SEQ = 256
T = META + SEQ
EPS = 1e-6
NEG = -1e30
NRAW = 4
NP = 7
AHEAD = 6
NH = 16
PAIR = 256

TILES = [(0, META), (META, META + P), (META + P, T)]

V_FFN1, V_MIX, V_FFN2, V_FINAL = 0, 16, 32, 48
W_FFN1, W_MIX, W_FFN2, W_CONV = 56, 72, 88, 104
V_GN, V_SUB, V_QG, V_KG = 128, 136, 138, 141
NVEC = 144


def constants():
    f = np.float32
    eye = np.eye(P, dtype=f)
    square = np.zeros((P, 5, P), f)
    square[:, 0] = eye
    square[:, 1] = eye - f(1.0 / P)
    square[:, 2] = 1.0 / P
    square[:, 3] = 1.0 / D
    square[:64, 4, :64] = 1.0 / 64
    square[64:, 4, 64:] = 1.0 / 64

    pos = np.arange(T, dtype=f)
    rot = np.zeros((P, 4, T), f)
    ang = (f(10000.0) ** (-np.linspace(0.0, 1.0, 64, dtype=f))).astype(f)
    fr = (pos[None, :] * ang[:, None]).astype(f).astype(np.float64)
    rot[0::2, 0] = rot[1::2, 0] = np.cos(fr)
    rot[0::2, 1] = -np.sin(fr)
    rot[1::2, 1] = np.sin(fr)
    inv = (f(500000.0) ** (-np.arange(0, 16, 2, dtype=f) / f(16))).astype(f)
    fr = (pos[None, :] * inv[:, None]).astype(f).astype(np.float64)
    rot[:, 2] = 1.0
    for b in (0, 64):
        rot[b:b + 8, 2] = rot[b + 8:b + 16, 2] = np.cos(fr)
        rot[b:b + 8, 3] = -np.sin(fr)
        rot[b + 8:b + 16, 3] = np.sin(fr)

    dec = np.zeros((P, 4, 384 + T), f)
    for h in range(4):
        lg = math.log(1.0 - 2.0 ** (-5.0 - h))

        def d(i, j):
            r = i - j
            return np.where(r >= 0, np.exp(lg * np.maximum(r, 0)), 0.0) * 128 ** -0.5
        a = np.arange(P)
        dec[:, h, 0:256] = d(np.arange(256)[None, :], a[:, None])
        dec[:, h, 256:384] = d(a[None, :], a[:, None])
        dec[:META, h, 384:] = d(np.arange(T)[None, :], np.arange(META)[:, None])

    mask = np.where(np.arange(T)[None, :] - (T - P) <= np.arange(P)[:, None], 0.0, NEG).astype(f)

    onehot = np.zeros((33, 3, 384), f)
    for g, (window, dil) in enumerate(((128, 1), (512, 4), (2048, 16))):
        n = window // dil
        for x in range(383):
            dist = 255 - x
            if dist >= 0 and dist % dil == 0 and dist // dil <= n:
                if dist < 16:
                    b = dist
                else:
                    v = np.log(f(dist) / f(16)) / f(math.log(2048 / 16)) * f(16)
                    b = min(16 + int(f(v)), 31)
                onehot[b, g, x] = 1.0
            else:
                onehot[32, g, x] = NEG
        onehot[32, g, 383] = NEG
    ones = np.ones((P, P), f)
    return {"c_square": square, "c_rot": rot, "c_dec0": dec[:, 0:2].copy(), "c_dec1": dec[:, 2:4].copy(), "c_mask": mask,
            "c_onehot": onehot, "c_ones": ones}


class Queues:

    ENGINES = ("pe", "act", "dve", "sp", "pool")

    def __init__(self):
        self.lists = {e: [] for e in self.ENGINES}
        self.count = {}

    def op(self, e, fn, *waits):
        self.count[e] = self.count.get(e, 0) + 1
        self.lists[e].append((waits, fn, (e, 1)))
        return e, self.count[e]

    def part(self, e, fn, *waits):
        self.lists[e].append((waits, fn, None))

    def wait(self, e, *waits):
        self.lists[e].append((waits, None, None))

    def dma(self, e, sem, out, in_, *waits):
        self.count[sem] = self.count.get(sem, 0) + 16
        self.lists[e].append((waits, lambda eng: eng.dma_start(out, in_), (sem, 16)))
        return sem, self.count[sem]

    def run(self, e, eng, sems):
        reached = {}
        for waits, fn, inc in self.lists[e]:
            for w in waits:
                if w is not None and reached.get(w[0], 0) < w[1]:
                    eng.wait_ge(sems[w[0]], w[1])
                    reached[w[0]] = w[1]
            if fn is not None:
                ins = fn(eng)
                if inc is not None:
                    ins.then_inc(sems[inc[0]], inc[1])


def build(nc, A, out):
    ctx = ExitStack()
    q = Queues()
    names = [0]

    def alloc(c, shape, dt=F32):
        names[0] += 1
        return c.enter_context(nc.sbuf_tensor(f"t{names[0]}", shape, dt))

    with ctx:
        raw = alloc(ctx, [P, NRAW, 8, PAIR])
        whi = alloc(ctx, [P, NP, 8, P], F32R)
        wlo = alloc(ctx, [P, NP, 8, P], F32R)
        h = alloc(ctx, [P, KC, T])
        xh = alloc(ctx, [P, KC, T], F32R)
        xl = alloc(ctx, [P, KC, T], F32R)
        acc = alloc(ctx, [P, T])
        sq = alloc(ctx, [P, 2, T])
        rs = alloc(ctx, [P, T])
        rstd = alloc(ctx, [P, T])
        vec = alloc(ctx, [P, NVEC])
        square = alloc(ctx, [P, 5, P])
        small = alloc(ctx, [P, 32])
        IDENT, CENTRE, MEAN, MEAND, MEAN64 = (square[:, i, :] for i in range(5))
        eps = small[:, 0:1]
        lamv = small[:, 4:8].rearrange("p (l m) -> p l m", l=2)
        subw = small[:, 8:10]
        qkg = small[:, 10:16]
        gn = small[:, 24:32]
        final = alloc(ctx, [P, 2, KC])

        ps = ctx.enter_context(nc.psum_tensor("ps", [P, 8, 512], F32))
        psa = ps[:, 4:8, :]
        scr = nc.dram_tensor("bias_rows", [NH, 3, 384], F32, kind="Internal")
        bands = nc.dram_tensor("bias_bands", [NH * 3, P, 256], F32, kind="Internal")

        def f32(ap):
            return ap.bitcast(F32)

        units, order = [], []

        def unit(w, r0, nk, col, n=PAIR):
            units.append((w, r0, nk, col, n))
            return len(units) - 1

        def pair_plan(a, b):
            order.extend([(a, 0), (b, 0), (a, 1), (b, 1)])

        def plan_ffn(gate, up, down):
            for i in range(F // PAIR):
                if not order:
                    for c in (0, P):
                        for w, first in (gate, up):
                            order.append((unit(w, 0, 8, first + c, P), 0))
                    continue
                a = unit(gate[0], 0, 8, gate[1] + i * PAIR)
                b = unit(up[0], 0, 8, up[1] + i * PAIR)
                pair_plan(a, b)
            for i in range(D // PAIR):
                us = [unit(down, r, n, i * PAIR) for r, n in ((0, 8), (1024, 8), (2048, 6))]
                for u in us:
                    order.extend([(u, 0), (u, 1)])

        def plan_cols(w, cols):
            for c in cols:
                u = unit(w, 0, 8, c)
                order.extend([(u, 0), (u, 1)])

        MIX_COLS = [PAIR * i for i in (8, 10, 12, 0, 2, 9, 4, 11, 13, 6, 1, 3, 5, 7)]
        DIL_SEQ = [(g, s) for g in range(3) for s in range(2)] + [(g, 2) for g in range(3)]
        OUT_COLS = [PAIR * i for i in range(4)]
        for l in range(2):
            plan_ffn((A["ffn1_w_gate"][l], 0), (A["ffn1_w_up"][l], 0), A["ffn1_w_down"][l])
            plan_cols(A["w_in"][l], MIX_COLS)
            plan_cols(A["w_out"][l], OUT_COLS)
            plan_ffn((A["ffn2_w_gate"][l], 0), (A["ffn2_w_up"][l], 0), A["ffn2_w_down"][l])
        for l in range(2):
            w = A["ffn1_w_in_2"][l]
            plan_ffn((w, 0), (w, F), A["ffn1_w_out_2"][l])
            if l == 0:
                w = A["conv_w_in_2"][0]
                for i in range(4):
                    a, b = unit(w, 0, 8, D + i * PAIR), unit(w, 0, 8, 2 * D + i * PAIR)
                    pair_plan(a, b)
                    plan_cols(w, [i * PAIR])
                plan_cols(A["conv_w_out_2"][0], OUT_COLS)
            else:
                for b in range(KC):
                    for g, s in DIL_SEQ:
                        order.append((unit(A["attn_w_qkv_2"][0], 0, 8, (3 * g + s) * D + b * P, P), 0))
                plan_cols(A["attn_w_out_2"][0], OUT_COLS)
            w = A["ffn2_w_in_2"][l]
            plan_ffn((w, 0), (w, F), A["ffn2_w_out_2"][l])

        loaded, halves = {}, {}
        highs, split, spent = [], [], []

        def load_unit(u, *waits):
            if u < len(units):
                w, r0, nk, col, n = units[u]
                src = w[r0:r0 + nk * P, col:col + n].rearrange("(k p) n -> p k n", p=P)
                loaded[u] = q.dma("sp", f"raw{u % NRAW}", raw[:, u % NRAW, 0:nk, 0:n], src, *waits)

        def high(ahead=NP):
            n = len(highs)
            if n >= len(order) or n >= len(spent) + ahead:
                return False
            u, half = order[n]
            nk = units[u][2]
            src = raw[:, u % NRAW, 0:nk, half * P:half * P + P]
            hi = whi[:, n % NP, 0:nk, :]
            highs.append(q.op("act", lambda e: e.activation(hi, src, ACT.Copy),
                              loaded[u], spent[n - NP] if n >= NP else None))
            return True

        def low():
            n = len(split)
            u, half = order[n]
            nk = units[u][2]
            src = raw[:, u % NRAW, 0:nk, half * P:half * P + P]
            hi, lo = whi[:, n % NP, 0:nk, :], wlo[:, n % NP, 0:nk, :]
            d = q.op("dve", lambda e: e.tensor_tensor(lo, src, f32(hi), ALU.subtract), highs[n])
            split.append(d)
            halves[u] = halves.get(u, 0) + 1
            if halves[u] * P == units[u][4]:
                load_unit(u + NRAW, d)

        def fill(ahead=AHEAD):
            got = high(ahead)
            if len(split) < len(highs) - got:
                low()

        bank_free = {}
        turn = [0]

        def use(*banks):
            pool[:] = banks
            turn[0] = 0

        def next_bank():
            turn[0] += 1
            return pool[(turn[0] - 1) % len(pool)]

        pool = []
        x_read = [None]

        def tiles(n, rhs, c0, hook=None):
            N = T - c0
            banks = [next_bank() for _ in range(n)]
            first = len(spent)
            left = {}
            for k, _ in rhs:
                left[k // 8] = left.get(k // 8, 0) + 1
            out_ = []
            for i, (k, get) in enumerate(rhs):
                if hook is not None:
                    hook(i)
                xhi, xlo, tok = get()
                group = first + k // 8 * n
                while len(split) < group + n:
                    if len(highs) == len(split):
                        high()
                    low()
                left[k // 8] -= 1
                for j in range(n):
                    piece = group + j
                    wh = whi[:, piece % NP, k % 8, :]
                    wl = wlo[:, piece % NP, k % 8, :]
                    o = ps[:, banks[j], 0:N]
                    start, stop = i == 0, i == len(rhs) - 1

                    def mm(e, wh=wh, wl=wl, o=o, start=start, stop=stop, xhi=xhi, xlo=xlo):
                        e.matmul(o, wh, xhi, start=start, stop=False)
                        e.matmul(o, wh, xlo, start=False, stop=False)
                        return e.matmul(o, wl, xhi, start=False, stop=stop)
                    waits = [tok, split[piece], bank_free.get(banks[j]) if start else None]
                    if stop or (left[k // 8] == 0 and j == n - 1):
                        t = q.op("pe", mm, *waits)
                    else:
                        q.part("pe", mm, *waits)
                    if stop:
                        out_.append((banks[j], t))
                if left[k // 8] == 0:
                    spent.extend([t] * n)
                    if not stop:
                        for _ in range(n):
                            fill()
            return out_

        xtok = [None] * KC

        def xs(c0):
            return [(k, lambda k=k: (xh[:, k, c0:T], xl[:, k, c0:T], xtok[k])) for k in range(KC)]

        acc_tok = [None]
        sq_read = [None, None]
        acc_read = [None]

        def post_chunk(m, tok, gcol, c0):
            g = vec[:, gcol + m:gcol + m + 1] if gcol != V_FINAL else final[:, 0, m:m + 1]
            hm = h[:, m, c0:T]
            a = q.op("act", lambda e: e.activation(xh[:, m, c0:T], hm, ACT.Copy, scale=g), tok, x_read[0])
            if m == 0:
                acc_tok[0] = q.op("act", lambda e: e.activation(acc[:, c0:T], hm, ACT.Square), acc_read[0])
            else:
                s = sq[:, m % 2, c0:T]
                b = q.op("act", lambda e: e.activation(s, hm, ACT.Square), sq_read[m % 2])
            xtok[m] = q.op("dve", lambda e: e.scalar_tensor_tensor(
                xl[:, m, c0:T], hm, g, f32(xh[:, m, c0:T]), ALU.mult, ALU.subtract), tok, a)
            if m:
                acc_tok[0] = sq_read[m % 2] = q.op("dve", lambda e: e.tensor_tensor(
                    acc[:, c0:T], acc[:, c0:T], s, ALU.add), b, acc_tok[0])

            if gcol == V_FINAL:
                gf = vec[:, V_FINAL + m:V_FINAL + m + 1]
                o = spare[0][:, 0 if m == 0 else 1 + m % 2, c0:T]
                b = q.op("act", lambda e: e.activation(o, hm, ACT.Square, scale=gf), sq2_read[m % 2])
                if m:
                    b = sq2_read[m % 2] = q.op("dve", lambda e: e.tensor_tensor(
                        spare[0][:, 0, c0:T], spare[0][:, 0, c0:T], o, ALU.add), b, acc2_tok[0])
                acc2_tok[0] = b

        spare, sq2_read, acc2_tok = [], [None, None], [None]
        table = [None]

        def log_exp():
            if table[0] != "log_exp":
                table[0] = "log_exp"
                q.part("act", lambda e: e.preload_act_table_set("natural_log_exp_and_others"))

        def silu(o, x, *waits):
            table[0] = "silu"
            return q.op("act", lambda e: e.activation(o, x, ACT.Silu), *waits)

        def root(ms, r, s, *waits):
            log_exp()
            a = q.op("act", lambda e: e.activation(s, ms, ACT.Ln, bias=eps), *waits)
            a = q.op("act", lambda e: e.activation(r, s, ACT.Exp, scale=-0.5), a)
            a = q.op("act", lambda e: e.activation(s, r, ACT.Square), a)
            d = q.op("dve", lambda e: e.scalar_tensor_tensor(s, ms, EPS, s, ALU.add, ALU.mult), a)
            return d, q.op("dve", lambda e: e.scalar_tensor_tensor(r, s, -3.0, r, ALU.add, ALU.mult), d)

        def norm_factor(c0):
            N = T - c0
            p = q.op("pe", lambda e: e.matmul(ps[:, 7, 0:N], MEAND, acc[:, c0:T], start=True, stop=True),
                     acc_tok[0], bank_free.get(7))
            acc_read[0] = p
            f, d = root(ps[:, 7, 0:N], rstd[:, c0:T], rs[:, c0:T], p, rs_read[0])
            bank_free[7] = f
            d = q.op("dve", lambda e: e.tensor_scalar(rstd[:, c0:T], rstd[:, c0:T], -0.5, None, ALU.mult), d)
            rs_read[0] = d
            return d

        rs_read = [None]
        side = deque()

        def final_norm(c0):
            u, r2 = spare[0][:, 3, c0:T], spare[1][:, 0, c0:T]
            r1, s = spare[0][:, 0, c0:T], rs[:, c0:T]
            N = T - c0
            ms1, ms2 = ps[:, 7, 0:N], ps[:, 6, 0:N]
            q.part("pe", lambda e: e.matmul(ms1, MEAND, acc[:, c0:T], start=True, stop=True),
                   acc_tok[0], bank_free.get(7))
            p = q.op("pe", lambda e: e.matmul(ms2, MEAND, spare[0][:, 0, c0:T], start=True, stop=True),
                     acc2_tok[0], bank_free.get(6))
            acc_read[0] = p
            f, d1 = root(ms1, r1, s, p, rs_read[0])
            bank_free[7] = f
            d = q.op("dve", lambda e: e.tensor_tensor(u, r1, r1, ALU.mult), d1)
            fill()
            bank_free[6] = d = q.op("dve", lambda e: e.scalar_tensor_tensor(u, ms2, 0.25, u, ALU.mult, ALU.mult), d)
            f, d = root(u, r2, s, d)
            d = rs_read[0] = q.op("dve", lambda e: e.scalar_tensor_tensor(
                rstd[:, c0:T], r1, 0.25, r2, ALU.mult, ALU.mult), d)
            read = "act", q.count["act"]

            def scale(m):
                q.op("dve", lambda e: e.scalar_tensor_tensor(
                    h[:, m, c0:T], h[:, m, c0:T], final[:, 1, m:m + 1], r1, ALU.mult, ALU.mult), d1, read)
            side.extend([lambda m=m: scale(m) for m in range(KC)])
            return d

        def first_tiles(n, c0, at=6, norm=norm_factor):
            r = []

            def hook(i):
                if i == at:
                    r.append(norm(c0))
            return tiles(n, xs(c0), c0, hook), r[0]

        def residual(c0, rhs, scale, gcol, groups, hook=None, banks=range(8)):
            use(*banks)
            m = 0
            for n in groups:
                ds = []
                made = tiles(n, rhs, c0, hook if m == 0 else None)
                for _ in range(2 * n):
                    fill(NP - n)
                while len(split) < len(highs):
                    low()
                for i, (b, t) in enumerate(made):
                    d = q.op("dve", lambda e, m=m + i, b=b: e.scalar_tensor_tensor(
                        h[:, m, c0:T], ps[:, b, 0:T - c0], scale, h[:, m, c0:T], ALU.mult, ALU.add), t)
                    bank_free[b] = d
                    ds.append(d)
                for d in ds:
                    if gcol is None:
                        store(m, d)
                    else:
                        post_chunk(m, d, gcol, c0)
                    m += 1
                for _ in range(2 * n):
                    fill()

        def store(m, d):
            done.append(q.dma("sp", "out", out[m * P:(m + 1) * P, :], h[:, m, META:T], d))

        done = []

        def phase_edge(*toks):
            for e in ("act", "dve"):
                q.wait(e, *((p, q.count.get(p, 0)) for p in ("pe", "act", "dve")), *toks)

        def silu_ffn(c0, gcol, first=False, norm=norm_factor):
            N = T - c0
            region = ExitStack()
            with region:
                ah = alloc(region, [P, FCH, T], F32R)
                al = alloc(region, [P, FCH, T], F32R)
                gs = alloc(region, [P, 2, T])
                sl = alloc(region, [P, 2, T])
                us = alloc(region, [P, 2, T])
            phase_edge()
            atok = [None] * FCH
            gs_read, sl_read, us_read = [None] * 2, [None] * 2, [None] * 2

            late = []

            def lows():
                while late:
                    late.pop(0)()

            def evac(j, G, U, r):
                (bg, tg), (bu, tu) = G, U
                i = j % 2
                d1 = q.op("dve", lambda e: e.tensor_tensor(gs[:, i, 0:N], ps[:, bg, 0:N], rstd[:, c0:T], ALU.mult),
                          tg, r, gs_read[i])
                bank_free[bg] = d1
                a1 = gs_read[i] = silu(sl[:, i, 0:N], gs[:, i, 0:N], d1, sl_read[i])
                lows()
                fill()
                d2 = q.op("dve", lambda e: e.tensor_tensor(us[:, i, 0:N], ps[:, bu, 0:N], rstd[:, c0:T], ALU.mult),
                          tu, us_read[i])
                bank_free[bu] = d2
                d3 = sl_read[i] = q.op("dve", lambda e: e.tensor_tensor(
                    us[:, i, 0:N], us[:, i, 0:N], sl[:, i, 0:N], ALU.mult), a1, d2)
                a2 = q.op("act", lambda e: e.activation(ah[:, j, 0:N], us[:, i, 0:N], ACT.Copy), d3)
                us_read[i] = a2
                fill()

                def rest():
                    atok[j] = q.op("dve", lambda e: e.tensor_tensor(
                        al[:, j, 0:N], us[:, i, 0:N], f32(ah[:, j, 0:N]), ALU.subtract), a2, d3)
                late.append(rest)

            use(*range(8))
            if first:
                b = tiles(2, xs(c0), c0)
                more, r = first_tiles(2, c0, 2)
                b += more
            else:
                b, r = first_tiles(4, c0, norm=norm)
            evac(0, b[0], b[1], r)
            evac(1, b[2], b[3], r)
            for j in range(2, FCH):
                if side:
                    side.popleft()()
                G = tiles(1, xs(c0), c0)[0]
                U = tiles(1, xs(c0), c0)[0]
                evac(j, G, U, r)
            lows()
            x_read[0] = ("pe", q.count["pe"])
            residual(c0, [(j, lambda j=j: (ah[:, j, 0:N], al[:, j, 0:N], atok[j])) for j in range(FCH)],
                     0.5, gcol, [2, 2, 2, 2])

        def mixer(l, gcol, consts, const_tok):
            rot, dec, mask = consts
            cq = 0 if l == 0 else META
            NQ = T - cq
            qt = TILES if l == 0 else TILES[1:]
            region = ExitStack()
            with region:
                qk = alloc(region, [P, 16, T])
                rotr = alloc(region, [P, 4, T])
                m1 = alloc(region, [P, 2, T])
                sh = alloc(region, [P, 2, T])
                vt = alloc(region, [P, 4, T])
                vk = alloc(region, [P, 3, 3, P])
                sm = alloc(region, [P, 2, T])
                tt = alloc(region, [P, T])
                st = alloc(region, [P, 24])
                lanes = [(alloc(region, [P, 384]), alloc(region, [META, T]), alloc(region, [P, T]),
                          alloc(region, [P, T]), alloc(region, [P, T])) for _ in range(2)]
                yh = alloc(region, [P, KC, T], F32R)
                yl = alloc(region, [P, KC, T], F32R)
            phase_edge()
            q.wait("dve", *const_tok)
            q.wait("pe", *const_tok)
            last = {}
            vmade = {}
            qtok, vtok, gtok, ytok = {}, {}, {}, [None] * KC
            swap2 = [i ^ 1 for i in range(32)]
            swap8 = [(i + 8) % 16 if i < 16 else i for i in range(32)]
            background = [deque(), deque(), deque()]
            count = [0]

            def step(lane):
                while background[lane]:
                    try:
                        next(background[lane][0])
                        return
                    except StopIteration:
                        background[lane].popleft()

            def steps():
                for lane in (2, 0, 1):
                    step(lane)

            def rotate(i, b, t, kind, c0):
                s = count[0] % 2
                count[0] += 1
                n = T - c0
                src = ps[:, b, 0:n]
                cos, sin = rotr[:, 2 * kind, c0:T], rotr[:, 2 * kind + 1, c0:T]
                d1 = q.op("dve", lambda e: e.stream_shuffle(sh[:, s, 0:n], src, swap8 if kind else swap2), t)
                d2 = q.op("dve", lambda e: e.tensor_tensor(m1[:, s, 0:n], src, cos, ALU.mult), rtok[1])
                bank_free[b] = d2
                d3 = q.op("dve", lambda e: e.tensor_tensor(sh[:, s, 0:n], sh[:, s, 0:n], sin, ALU.mult), d1)
                fill()
                qtok[i] = q.op("dve", lambda e: e.tensor_tensor(qk[:, i, c0:T], m1[:, s, 0:n], sh[:, s, 0:n], ALU.add), d3)

            def values(i, b, t):
                v = i % 4
                if i >= 4:
                    assert ("vt", v) in last
                d = q.op("dve", lambda e: e.tensor_tensor(vt[:, v, :], ps[:, b, 0:T], rstd[:, :], ALU.mult),
                         t, last.get(("vt", v)))
                bank_free[b] = d
                vmade[i] = len(spent)
                vtok[i] = d

            def gate(i, b, t):
                g = qk[:, 8 + i, cq:T]
                d = q.op("dve", lambda e: e.tensor_tensor(g, ps[:, b, 0:NQ], rstd[:, cq:T], ALU.mult),
                         t, last["scored", i])
                bank_free[b] = d
                gtok[i] = silu(g, g, d)

            def token_major(i, basis, bank):
                s = heads[0] % 3
                heads[0] += 1
                o = ps[:, bank, :]

                def mm(e):
                    for k, (a, z) in enumerate(TILES):
                        x = e.matmul(o[0:z - a, k * P:(k + 1) * P], vt[:, i % 4, a:z], basis,
                                     start=True, stop=True)
                    return x
                p = last["vt", i % 4] = q.op("pe", mm, vtok[i], bank_free.get(bank))
                q.op("act", lambda e: e.activation(vk[:, s, 1:3, :], o[:, P:3 * P].rearrange(
                    "p (k n) -> p k n", k=2), ACT.Copy), p, last.get(("vk", s)))
                a = q.op("act", lambda e: e.activation(vk[0:META, s, 0, :], o[0:META, 0:P], ACT.Copy))
                bank_free[bank] = a
                return s, a

            heads = [0]

            def mix_values(s, w12, w0, bank, *toks):
                def mm(e):
                    o = ps[:, bank, :]
                    e.matmul(o[:, 0:NQ], vk[0:META, s, 0, :], w0[:, cq:T], start=True, stop=False)
                    a = META - cq
                    e.matmul(o[:, a:NQ], vk[:, s, 1, :], w12[:, 0:256], start=False, stop=False)
                    return e.matmul(o[:, a + P:NQ], vk[:, s, 2, :], w12[:, 256:384], start=False, stop=True)
                p = last["vk", s] = q.op("pe", mm, *toks, bank_free.get(bank))
                return p

            def normalise(lane, bank, p, w, other):
                o2, rv, y = lanes[lane][2:]
                o = ps[:, bank, 0:NQ]
                ms = ps[:, other, 0:NQ]
                a = q.op("act", lambda e: e.activation(o2[:, 0:NQ], o, ACT.Square), p, last.get(("o2", lane)))
                yield
                m = q.op("pe", lambda e: e.matmul(ms, MEAN, o2[:, 0:NQ], start=True, stop=True),
                         a, bank_free.get(other))
                f, d = root(ms, rv[:, 0:NQ], o2[:, 0:NQ], m, last.get(("rv", lane)))
                bank_free[other] = f
                last["o2", lane] = d
                d = q.op("dve", lambda e: e.scalar_tensor_tensor(y[:, 0:NQ], o, w, rv[:, 0:NQ], ALU.mult, ALU.mult),
                         d, last.get(("y", lane)))
                last["rv", lane] = d
                bank_free[bank] = d
                last["made", lane] = d

            def emit_y(lane, c, d):
                y = lanes[lane][4]
                a = last["y", lane] = q.op("act", lambda e: e.activation(yh[:, c, cq:T], y[:, 0:NQ], ACT.Copy), d)
                fill()
                ytok[c] = q.op("dve", lambda e: e.tensor_tensor(yl[:, c, cq:T], y[:, 0:NQ],
                                                                f32(yh[:, c, cq:T]), ALU.subtract), a, d)

            def diff_head(i):
                aT, aT0 = lanes[0][0:2]
                qi, ki = 8 + i, 12 + i
                col = {0: META + P, META: 0, META + P: 0}

                def softmax(group):
                    def scores(e):
                        for a, z in group:
                            for m in range(2):
                                x = e.matmul(ps[0:z - a, 4 + m, col[a]:col[a] + z],
                                             qk[64 * m:64 * m + 64, qi, a:z],
                                             qk[64 * m:64 * m + 64, ki, 0:z], start=True, stop=True)
                        return x
                    p = last["scored", i] = q.op("pe", scores, qtok[qi], qtok[ki], bank_free.get(4), bank_free.get(5))
                    made = {}
                    for n, (a, z) in enumerate(group):
                        r, c, v = z - a, slice(col[a], col[a] + z), 12 * n
                        mk = mask[0:r, T - z:T] if r == P else mask[0:r, T - P:T - P + z]
                        for m in range(2):
                            d = q.op("dve", lambda e, m=m, r=r, c=c, v=v, mk=mk: e.tensor_tensor_reduce(
                                out=sm[0:r, m, c], in0=ps[0:r, 4 + m, c], in1=mk, scale=1.0, scalar=-3.0e38,
                                op0=ALU.add, op1=ALU.max, accum_out=st[0:r, v + m:v + m + 1]), p)
                        d = q.op("dve", lambda e, r=r, v=v: e.tensor_scalar(
                            st[0:r, v + 2:v + 4], st[0:r, v:v + 2], -0.125, None, ALU.mult), d)
                        log_exp()
                        for m in range(2):
                            x = q.op("act", lambda e, m=m, r=r, c=c, v=v: e.activation(
                                sm[0:r, m, c], sm[0:r, m, c], ACT.Exp, bias=st[0:r, v + 2 + m:v + 3 + m],
                                scale=0.125, accum_out=st[0:r, v + 4 + m:v + 5 + m]), d)
                        made[a] = x
                    bank_free[4] = bank_free[5] = d
                    fill()
                    for n, (a, z) in enumerate(group):
                        r, c, v = z - a, slice(col[a], col[a] + z), 12 * n
                        d = q.op("dve", lambda e, r=r, v=v: e.reciprocal(st[0:r, v + 6:v + 8], st[0:r, v + 4:v + 6]),
                                 made[a])
                        d = q.op("dve", lambda e, r=r, v=v: e.tensor_tensor(
                            st[0:r, v + 8:v + 10], st[0:r, v + 6:v + 8], lamv[0:r, l, :], ALU.mult), d)
                        d = q.op("dve", lambda e, r=r, c=c, v=v: e.tensor_scalar(
                            sm[0:r, 1, c], sm[0:r, 1, c], st[0:r, v + 9:v + 10], None, ALU.mult), d)
                        d = q.op("dve", lambda e, r=r, c=c, v=v: e.scalar_tensor_tensor(
                            tt[0:r, c], sm[0:r, 0, c], st[0:r, v + 8:v + 9], sm[0:r, 1, c], ALU.mult, ALU.add),
                            d, last.get("tt"))
                    return d

                def turn_over(group, d):
                    def mm(e):
                        for a, z in group:
                            r, c = z - a, col[a]
                            x = e.matmul(ps[0:META, 7, a:z], tt[0:r, c:c + META], IDENT[0:r, 0:r], start=True, stop=True)
                            if a >= META:
                                x = e.transpose(ps[:, 6, a - META:z - META], tt[0:r, c + META:c + META + P], IDENT)
                            if a >= META + P:
                                x = e.transpose(ps[:, 6, 256:384], tt[0:r, c + META + P:c + T], IDENT)
                        return x
                    last["tt"] = q.op("pe", mm, d, bank_free.get(6), bank_free.get(7))

                d = softmax(qt[:-1])
                yield
                while i not in vtok or len(spent) == vmade[i]:
                    yield
                s, _ = token_major(i, IDENT, 7)
                yield
                yield
                if i == 0:
                    yield
                assert not background[2]
                turn_over(qt[:-1], d)
                d = softmax(qt[-1:])
                yield
                yield
                turn_over(qt[-1:], d)
                p = last["tt"]
                x0 = q.op("act", lambda e: e.activation(aT[:, :], ps[:, 6, 0:384], ACT.Copy), p, last.get(("aT", 0)))
                x1 = q.op("act", lambda e: e.activation(aT0[:, cq:T], ps[0:META, 7, cq:T], ACT.Copy))
                bank_free[6] = x0
                bank_free[7] = x1
                background[2].append(diff_out(i, s, x1))

            def diff_out(i, s, x1):
                aT, aT0 = lanes[0][0:2]
                p = last["aT", 0] = mix_values(s, aT, aT0, 6, x1)
                yield from normalise(0, 6, p, subw[:, l:l + 1], 7)
                emit_y(0, 4 + i, last["made", 0])

            def ret_head(i, lane):
                aT, aT0 = lanes[lane][0:2]
                bank, other = ((6, 7), (2, 3))[lane]
                while len(spent) == vmade[4 + i] or (lane == 0 and background[2]):
                    yield
                if lane == 0:
                    yield
                    yield
                s, vdone = token_major(4 + i, CENTRE, bank)
                qi, ki = i, 4 + i
                p = q.op("pe", lambda e: e.matmul(ps[0:META, other, 0:NQ], qk[:, ki, 0:META], qk[:, qi, cq:T],
                                                  start=True, stop=True), qtok[qi], qtok[ki], bank_free.get(other))
                x0 = q.op("dve", lambda e: e.tensor_tensor(aT0[:, cq:T], ps[0:META, other, 0:NQ],
                                                           dec[0:META, i, 384 + cq:384 + T], ALU.mult),
                          p, last.get(("aT", lane)))
                bank_free[other] = x0
                yield

                def scores(e):
                    e.matmul(ps[:, other, 0:256], qk[:, ki, META:META + P], qk[:, qi, META:T], start=True, stop=True)
                    return e.matmul(ps[:, other, 256:384], qk[:, ki, META + P:T], qk[:, qi, META + P:T],
                                    start=True, stop=True)
                p = q.op("pe", scores, bank_free[other])
                d = q.op("dve", lambda e: e.tensor_tensor(aT[:, :], ps[:, other, 0:384], dec[:, i, 0:384], ALU.mult), p)
                bank_free[other] = d
                yield
                if i < 2:
                    yield
                p = last["aT", lane] = mix_values(s, aT, aT0, bank, d, vdone)
                yield from normalise(lane, bank, p, gn[:, 4 * l + i:4 * l + i + 1], other)
                while i not in gtok:
                    yield
                y = lanes[lane][4]
                d = q.op("dve", lambda e: e.tensor_tensor(y[:, 0:NQ], y[:, 0:NQ], qk[:, 8 + i, cq:T], ALU.mult),
                         gtok[i], last["made", lane])
                emit_y(lane, i, d)
                yield

            kinds = [("dq", 0), ("dk", 0), ("dv", 0), ("rq", 0), ("rk", 0), ("dq", 2), ("rv", 0), ("dk", 2),
                     ("dv", 2), ("rg", 0), ("rq", 2), ("rk", 2), ("rv", 2), ("rg", 2)]
            RET_LANE = [1, 1, 1, 0]
            rtok = [None, None]

            def evac(kind, i, b, t):
                if kind == "dq":
                    rotate(8 + i, b, t, 1, cq)
                elif kind == "dk":
                    rotate(12 + i, b, t, 1, 0)
                    background[0].append(diff_head(i))
                elif kind == "rq":
                    rotate(i, b, t, 0, cq)
                elif kind == "rk":
                    rotate(4 + i, b, t, 0, 0)
                elif kind == "dv":
                    values(i, b, t)
                elif kind == "rv":
                    values(4 + i, b, t)
                    background[RET_LANE[i]].append(ret_head(i, RET_LANE[i]))
                else:
                    gate(i, b, t)

            start = {"dq": cq, "rq": cq, "rg": cq}
            assert cq == 0 or start["dq"] == META
            use(0, 1, 2, 3)
            b = tiles(2, xs(cq), cq)
            more, r = first_tiles(2, 0, 2)
            b += more
            rtok[0] = r

            def rotation(kind):
                for j in (2 * kind, 2 * kind + 1):
                    rtok[1] = q.op("dve", lambda e, j=j: e.tensor_tensor(
                        rotr[:, j, :], rot[:, j, :], rstd[:, :], ALU.mult), r)
            rotation(1)
            for j, (bk, t) in enumerate(b):
                evac(kinds[j // 2][0], kinds[j // 2][1] + j % 2, bk, t)
            for kind, i in kinds[2:]:
                if (kind, i) == ("rv", 0):
                    use(0, 1)
                if (kind, i) == ("rq", 0):
                    rotation(0)
                for j in range(2):
                    c0 = start.get(kind, 0)
                    bk, t = tiles(1, xs(c0), c0)[0]
                    evac(kind, i + j, bk, t)
                    fill()
                    steps()
            x_read[0] = ("pe", q.count["pe"])
            while None in ytok[4:]:
                steps()

            def hook(i):
                steps()
                while ytok[ks[i]] is None:
                    steps()
            ks = [4, 5, 6, 7, 0, 1, 2, 3]
            residual(cq, [(k, lambda k=k: (yh[:, k, cq:T], yl[:, k, cq:T], ytok[k])) for k in ks],
                     1.0, gcol, [4, 1, 1, 1, 1], hook, (0, 1, 4, 5, 2, 3, 6, 7))

        def conv_mixer(gcol):
            c0 = META
            region = ExitStack()
            with region:
                cs = alloc(region, [P, 2, SEQ])
                us = alloc(region, [P, 2, SEQ])
                vp = alloc(region, [P, 2, SEQ + 2])
                cv = alloc(region, [P, 4, SEQ])
                y = alloc(region, [P, 2, SEQ])
                yh = alloc(region, [P, KC, SEQ], F32R)
                yl = alloc(region, [P, KC, SEQ], F32R)
            phase_edge()
            z = q.op("dve", lambda e: e.memset(vp[:, :, 0:2], 0.0))
            ytok, cvtok, yread = [None] * KC, [None] * KC, [None] * 2
            r = [None]

            def conv(j, C, U):
                i = j % 2
                d1 = q.op("dve", lambda e: e.tensor_tensor(cs[:, i, :], ps[:, C[0], 0:SEQ], rstd[:, c0:T], ALU.mult),
                          C[1], r[0])
                bank_free[C[0]] = d1
                fill()
                lows()
                d2 = q.op("dve", lambda e: e.tensor_tensor(us[:, i, :], ps[:, U[0], 0:SEQ], rstd[:, c0:T], ALU.mult), U[1])
                bank_free[U[0]] = d2
                d3 = q.op("dve", lambda e: e.tensor_tensor(vp[:, i, 2:], cs[:, i, :], us[:, i, :], ALU.mult), d2)
                o = cv[:, j % 4, :]
                d = q.op("dve", lambda e: e.tensor_scalar(o, vp[:, i, 2:], vec[:, W_CONV + j:W_CONV + j + 1],
                                                          None, ALU.mult), d3, z)
                fill()
                for lag in (1, 2):
                    w = vec[:, W_CONV + 8 * lag + j:W_CONV + 8 * lag + j + 1]
                    d = q.op("dve", lambda e, lag=lag, w=w: e.scalar_tensor_tensor(
                        o, vp[:, i, 2 - lag:2 - lag + SEQ], w, o, ALU.mult, ALU.add), d)
                cvtok[j] = d

            late = []

            def lows():
                while late:
                    late.pop(0)()

            def gate(j, B):
                i = j % 2
                lows()
                d = q.op("dve", lambda e: e.tensor_tensor(y[:, i, :], ps[:, B[0], 0:SEQ], rstd[:, c0:T], ALU.mult),
                         B[1], yread[i])
                bank_free[B[0]] = d
                d = q.op("dve", lambda e: e.tensor_tensor(y[:, i, :], y[:, i, :], cv[:, j % 4, :], ALU.mult), d, cvtok[j])
                a = q.op("act", lambda e: e.activation(yh[:, j, :], y[:, i, :], ACT.Copy), d)
                fill()

                def rest():
                    yread[i] = ytok[j] = q.op("dve", lambda e: e.tensor_tensor(
                        yl[:, j, :], y[:, i, :], f32(yh[:, j, :]), ALU.subtract), a)
                late.append(rest)

            for i in range(4):
                if i == 0:
                    use(*range(8))
                    b, r[0] = first_tiles(4, c0)
                    conv(0, b[0], b[1])
                    conv(1, b[2], b[3])
                else:
                    for j in range(2):
                        C = tiles(1, xs(c0), c0)[0]
                        U = tiles(1, xs(c0), c0)[0]
                        conv(2 * i + j, C, U)
                for j in range(2):
                    gate(2 * i + j, tiles(1, xs(c0), c0)[0])
            lows()
            x_read[0] = ("pe", q.count["pe"])
            residual(c0, [(k, lambda k=k: (yh[:, k, :], yl[:, k, :], ytok[k])) for k in range(KC)],
                     1.0, gcol, [3, 1, 1, 1, 1, 1])

        def dilated_mixer(gcol, band_tok):
            c0 = META
            region = ExitStack()
            with region:
                qk = alloc(region, [P, 2, 3, 2, SEQ])
                vt = alloc(region, [P, 3, SEQ])
                vk = alloc(region, [P, 2, 2, 3, P])
                sqb = alloc(region, [P, 3, 512])
                rq = alloc(region, [P, 512])
                rt = alloc(region, [P, 512])
                bias = alloc(region, [P, 2, 3, 256])
                p1s = alloc(region, [P, 2, 3, 256])
                p0s = alloc(region, [P, 2, 3, P])
                pTs = alloc(region, [P, 2, 3, 384])
                sts = alloc(region, [P, 2, 8])
                yh = alloc(region, [P, KC, SEQ], F32R)
                yl = alloc(region, [P, KC, SEQ], F32R)
            phase_edge()
            q.wait("pool", ("pe", q.count["pe"]), ("act", q.count["act"]), ("dve", q.count["dve"]))
            last, ytok = {}, [None] * KC
            qktok, vktok = {}, {}
            bias_tok = {}

            def load_bias(n, *waits):
                if n < NH:
                    src = bands.ap()[3 * n:3 * n + 3].rearrange("g i x -> i g x")
                    bias_tok[n] = q.dma("pool", f"bias{n % 2}", bias[:, n % 2, :, :], src, band_tok, *waits)

            load_bias(0)
            load_bias(1)

            slot = [0]
            due = {}

            def advance(g):
                step = next(g, None)
                if step is not None:
                    due.setdefault((slot[0] + step[0], step[1]), []).append(g)

            def stages(phase):
                for g in due.pop((slot[0], phase), []):
                    advance(g)

            aux, aux_busy = deque(), [False]
            heads, lane_free = deque(), [0, 0]
            tiles_left = [9 * KC]

            def begin():
                if aux and not aux_busy[0] and aux[0][0] <= slot[0]:
                    aux_busy[0] = True
                    advance(aux.popleft()[1])
                for lane in range(1 if tiles_left[0] else 2):
                    if heads and lane_free[lane] <= slot[0] and (heads[0] // 2, 2) in qktok:
                        lane_free[lane] = slot[0] + 4
                        advance(head(heads.popleft(), lane))

            def end_slot():
                stages("late")
                stages("pe")
                begin()
                slot[0] += 1

            def head(n, lane):
                b, r = n // 2, n % 2
                rows = slice(64 * r, 64 * r + 64)
                base = (4, 0)[lane]
                B = bias[:, n % 2, :, :]
                p1, p0, pT, st = p1s[:, lane], p0s[:, lane], pTs[:, lane], sts[:, lane]
                s1 = ps[:, base:base + 2, :].rearrange("p b n -> p (b n)")[:, 0:768].rearrange(
                    "p (g n) -> p g n", g=3)
                s0 = ps[:, base + 2, 0:384].rearrange("p (g n) -> p g n", g=3)
                o = ps[rows, base + 3, 0:SEQ]

                def Q(g, s):
                    return qk[rows, b % 2, g, s, :]

                def scores(e):
                    for g in range(3):
                        e.matmul(s1[:, g, :], Q(g, 0)[:, P:SEQ], Q(g, 1), start=True, stop=True)
                    for g in range(3):
                        x = e.matmul(s0[:, g, :], Q(g, 0)[:, 0:P], Q(g, 1)[:, 0:P], start=True, stop=True)
                    return x
                p = q.op("pe", scores, qktok[b, 2], *(bank_free.get(base + i) for i in range(3)))
                last["qk", b % 2] = p
                yield 1, "early"
                d1 = q.op("dve", lambda e: e.tensor_tensor_reduce(
                    out=p1, in0=s1, in1=B, scale=1.0, scalar=-3.0e38, op0=ALU.add, op1=ALU.max,
                    accum_out=st[:, 0:1]), p, bias_tok[n], last.get(("p", lane)))
                d0 = q.op("dve", lambda e: e.tensor_tensor_reduce(
                    out=p0, in0=s0, in1=B[:, :, P:256], scale=1.0, scalar=-3.0e38, op0=ALU.add, op1=ALU.max,
                    accum_out=st[:, 1:2]))
                load_bias(n + 2, d0)
                d = q.op("dve", lambda e: e.tensor_scalar(st[:, 2:4], st[:, 0:2], -1.0, None, ALU.mult), d0)
                log_exp()
                q.op("act", lambda e: e.activation(p1, p1, ACT.Exp, bias=st[:, 2:3], accum_out=st[:, 4:5]), d)
                a = q.op("act", lambda e: e.activation(p0, p0, ACT.Exp, bias=st[:, 3:4], accum_out=st[:, 5:6]))
                yield 1, "early"
                d = q.op("dve", lambda e: e.reciprocal(st[:, 6:8], st[:, 4:6]), a)
                q.op("dve", lambda e: e.tensor_scalar(p1, p1, st[:, 6:7], None, ALU.mult), d)
                d = q.op("dve", lambda e: e.tensor_scalar(p0, p0, st[:, 7:8], None, ALU.mult))
                yield 1, "pe"

                def turn_over(e):
                    for g in range(3):
                        e.transpose(s0[:, g, :], p0[:, g, :], IDENT)
                    for g in range(3):
                        for j in range(2):
                            x = e.transpose(s1[:, g, j * P:(j + 1) * P], p1[:, g, j * P:(j + 1) * P], IDENT)
                    return x
                p = last["p", lane] = q.op("pe", turn_over, d)
                yield 1, "early"
                q.op("act", lambda e: e.activation(pT[:, :, 0:P], s0, ACT.Copy), p, last.get(("pT", lane)))
                a = q.op("act", lambda e: e.activation(pT[:, :, P:384], s1, ACT.Copy))
                bank_free[base] = bank_free[base + 1] = bank_free[base + 2] = a
                yield 1, "pe"
                while (b, 2) not in vktok:
                    yield 1, "pe"

                def mix(e):
                    c = slice(64 * r, 64 * r + 64)
                    for g in range(3):
                        e.matmul(o, vk[:, b % 2, 0, g, c], pT[:, g, 0:256], start=g == 0, stop=False)
                    for g in range(3):
                        x = e.matmul(o[:, P:SEQ], vk[:, b % 2, 1, g, c], pT[:, g, 256:384], start=False, stop=g == 2)
                    return x
                p = last["pT", lane] = last["vk", b % 2] = q.op("pe", mix, a, vktok[b, 2], bank_free.get(base + 3))
                yield 1, "early"
                a = q.op("act", lambda e: e.activation(yh[rows, b, :], o, ACT.Copy), p)
                yield 0, "late"
                bank_free[base + 3] = ytok[b] = q.op("dve", lambda e: e.tensor_tensor(
                    yl[rows, b, :], o, f32(yh[rows, b, :]), ALU.subtract), a)

            def qk_norm(b, g, i, sq_tok):
                p = last["sqr", i] = q.op("pe", lambda e: e.matmul(
                    ps[:, 3, :], MEAN64, sqb[:, i, :], start=True, stop=True), sq_tok, bank_free.get(3))
                yield 1, "early"
                log_exp()
                a = q.op("act", lambda e: e.activation(rt[:, :], ps[:, 3, :], ACT.Ln, bias=eps), p, last.get("rt"))
                a = q.op("act", lambda e: e.activation(rq[:, :], rt[:, :], ACT.Exp, scale=-0.5), a, last.get("rq"))
                a = q.op("act", lambda e: e.activation(rt[:, :], rq[:, :], ACT.Square), a)
                yield 0, "late"
                d = q.op("dve", lambda e: e.scalar_tensor_tensor(
                    rt[:, :], ps[:, 3, :], EPS, rt[:, :], ALU.add, ALU.mult), a)
                bank_free[3] = d
                aux_busy[0] = False
                d = q.op("dve", lambda e: e.scalar_tensor_tensor(
                    rq[:, :], rt[:, :], -3.0, rq[:, :], ALU.add, ALU.mult), d)
                last["rt"] = d
                for s in range(2):
                    o = qk[:, b % 2, g, s, :]
                    last["rq"] = qktok[b, g] = q.op("dve", lambda e, o=o, s=s: e.scalar_tensor_tensor(
                        o, o, qkg[:, 3 * s + g:3 * s + g + 1], rq[:, s * SEQ:(s + 1) * SEQ], ALU.mult, ALU.mult), d)

            def v_turn(b, g, d):
                def mm(e):
                    for j in range(2):
                        x = e.transpose(ps[:, 3, j * P:(j + 1) * P], vt[:, g, j * P:(j + 1) * P], IDENT)
                    return x
                p = last["vt", g] = q.op("pe", mm, d, bank_free.get(3))
                yield 1, "early"
                bank_free[3] = vktok[b, g] = q.op("act", lambda e: e.activation(
                    vk[:, b % 2, :, g, :], ps[:, 3, 0:256].rearrange("p (j n) -> p j n", j=2), ACT.Copy),
                    p, last.get(("vk", b % 2)))
                aux_busy[0] = False

            norms = [0]

            def evac(b, g, s, bk, t, *waits):
                src = ps[:, bk, 0:SEQ]
                if s < 2:
                    i = norms[0] % 3
                    o = qk[:, b % 2, g, s, :]
                    d = q.op("dve", lambda e: e.tensor_tensor(o, src, rstd[:, c0:T], ALU.mult),
                             t, last.get(("qk", b % 2)), *waits)
                    a = q.op("act", lambda e: e.activation(sqb[:, i, s * SEQ:(s + 1) * SEQ], o, ACT.Square),
                             d, last.get(("sqr", i)))
                    if s:
                        norms[0] += 1
                        aux.append((slot[0] + 1 + (b == 0), qk_norm(b, g, i, a)))
                else:
                    d = q.op("dve", lambda e: e.tensor_tensor(vt[:, g, :], src, rstd[:, c0:T], ALU.mult),
                             t, last.get(("vt", g)), *waits)
                    aux.append((slot[0] + 2, v_turn(b, g, d)))
                bank_free[bk] = d

            use(0, 1, 2, 3)
            ready, r = first_tiles(4, c0)
            use(0, 1, 2)
            for b in range(KC):
                for g, s in DIL_SEQ:
                    if ready:
                        tile = ready.pop(0)
                    else:
                        tile = tiles(1, xs(c0), c0)[0]
                        fill()
                    tiles_left[0] -= 1
                    stages("early")
                    evac(b, g, s, *tile, r)
                    fill()
                    if len(ready) == 0:
                        end_slot()
                heads.extend([2 * b, 2 * b + 1])
            while due or aux or heads:
                stages("early")
                end_slot()
            x_read[0] = ("pe", q.count["pe"])
            residual(c0, [(k, lambda k=k: (yh[:, k, :], yl[:, k, :], ytok[k])) for k in range(KC)],
                     1.0, gcol, [3, 1, 1, 1, 1, 1])

        vectok = q.dma("sp", "vec", vec[:, :], A["vec"])
        htok = [q.dma("sp", f"h{i}", h[:, 4 * i:4 * i + 4, :],
                      A["hT"][512 * i:512 * i + 512].rearrange("(k p) t -> p k t", p=P)) for i in range(2)]
        log_exp()
        sqtok = q.dma("pool", "sqc", square[:, :, :], A["c_square"])
        for u in range(NRAW):
            load_unit(u)
        e0 = q.op("dve", lambda e: e.memset(small[:, :], 0.0))
        e0 = q.op("dve", lambda e: e.memset(eps, EPS), e0)
        e0 = q.op("dve", lambda e: e.memset(lamv[:, :, 0:1], 1.0), e0)
        q.wait("act", vectok, e0)
        q.wait("dve", vectok)
        q.wait("pe", sqtok)

        block1 = ExitStack()
        with block1:
            rot = alloc(block1, [P, 4, T])
            dec = alloc(block1, [P, 4, 384 + T])
            mask = alloc(block1, [P, T])
            d = q.op("dve", lambda e: e.tensor_tensor(
                final[:, 0, :], vec[:, V_FINAL:V_FINAL + KC], vec[:, W_FFN1:W_FFN1 + KC], ALU.mult))
            d = q.op("dve", lambda e: e.tensor_scalar(final[:, 1, :], vec[:, V_FINAL:V_FINAL + KC], -0.5, None, ALU.mult))
            q.wait("act", d)
            q.wait("dve", d)
            for m in range(KC):
                post_chunk(m, htok[m // 4], V_FFN1, 0)
                if m % 2:
                    fill()
            start = ExitStack()
            with start:
                oh = alloc(start, [33, 3, 384])
                rb = alloc(start, [33, 48])
                eb = alloc(start, [NH, 3, 384])
                lam = alloc(start, [64, 16])
                ones = alloc(start, [P, P])

                def load_start():
                    w = "pe", q.count["pe"]
                    itok.extend([q.dma("pool", "init", oh[:, :, :], A["c_onehot"], w),
                                 q.dma("pool", "init", rb[0:32, :], A["rel_bias_2"]),
                                 q.dma("pool", "init", rb[32:33, :], A["c_ones"][0:1, 0:48]),
                                 q.dma("pool", "init", lam[:, 0:8], A["lam"]),
                                 q.dma("pool", "init", ones[:, :], A["c_ones"])])

                def load_const(o, name):
                    consts.append(q.dma("pool", "const", o, A[name], ("pe", q.count["pe"])))

                def start_work():
                    d = q.op("dve", lambda e: e.tensor_tensor(lam[:, 8:12], lam[:, 0:4], lam[:, 4:8], ALU.mult), itok[-1])

                    def start_mm(e):
                        e.matmul(psa[:, 3, 0:4], ones[0:64, :], lam[:, 8:12], start=True, stop=True)
                        for g in range(3):
                            x = e.matmul(psa[0:NH, g, 0:384], rb[:, 16 * g:16 * g + 16], oh[:, g, :], start=True, stop=True)
                        return x
                    p = q.op("pe", start_mm, d, itok[-1], *(bank_free.get(i) for i in range(4, 8)))
                    for g in range(3):
                        dd = q.op("dve", lambda e, g=g: e.tensor_copy(eb[:, g, :], psa[0:NH, g, 0:384]), p)
                    bank_free[4] = bank_free[5] = bank_free[6] = dd
                    scr_tok.append(q.dma("pool", "scr", scr.ap(), eb[:, :, :], dd))

                    log_exp()
                    a = q.op("act", lambda e: e.activation(small[:, 16:20], psa[:, 3, 0:4], ACT.Exp), p)
                    bank_free[7] = a
                    for l in range(2):
                        li = 0.8 - 0.6 * math.exp(-0.3 * l)
                        d = q.op("dve", lambda e, l=l: e.tensor_tensor(
                            small[:, 20 + l:21 + l], small[:, 18 + l:19 + l], small[:, 16 + l:17 + l], ALU.subtract), a)
                        d = q.op("dve", lambda e, l=l, li=li: e.tensor_scalar(
                            lamv[:, l, 1:2], small[:, 20 + l:21 + l], -li, None, ALU.add), d)
                        d = q.op("dve", lambda e, l=l, li=li: e.tensor_scalar(
                            subw[:, l:l + 1], vec[:, V_SUB + l:V_SUB + l + 1], -0.5 * (1.0 - li), None, ALU.mult))
                    d = q.op("dve", lambda e: e.tensor_scalar(qkg[:, 0:3], vec[:, V_QG:V_QG + 3], -0.0625, None, ALU.mult))
                    d = q.op("dve", lambda e: e.tensor_scalar(qkg[:, 3:6], vec[:, V_KG:V_KG + 3], -0.5, None, ALU.mult))
                    d = q.op("dve", lambda e: e.tensor_scalar(gn, vec[:, V_GN:V_GN + 8], -0.5, None, ALU.mult))
                    q.wait("dve", d)

                itok, consts, scr_tok = [], [], []
                side.extend([load_start, lambda: load_const(rot[:, :, :], "c_rot"),
                             lambda: load_const(dec[:, 0:2, :], "c_dec0"), lambda: load_const(dec[:, 2:4, :], "c_dec1"),
                             lambda: load_const(mask[:, :], "c_mask"), lambda: None, lambda: None,
                             start_work])
                silu_ffn(0, V_MIX, True)
            assert not side
            def make_bands(n):
                w = q.dma("pool", "bands", bands.ap()[3 * n:3 * n + 3],
                          bass.AP(scr, 127 + 1152 * n, [[384, 3], [-1, P], [1, 256]]), scr_tok[0], ("pe", q.count["pe"]))
                band_tok[:] = [w]

            band_tok = []
            q.wait("act", *scr_tok)
            q.wait("dve", *scr_tok)
            side.extend([lambda n=n: make_bands(n) for n in range(NH)])

            mixer(0, V_FFN2, (rot, dec, mask), [consts[-1]])
            silu_ffn(0, V_FFN1 + 8)
            silu_ffn(0, V_MIX + 8)
            mixer(1, V_FFN2 + 8, (rot, dec, mask), [])
            spare.extend([rot, mask[:, None, :]])
            silu_ffn(META, V_FINAL)
            silu_ffn(META, W_MIX, norm=final_norm)
        conv_mixer(W_FFN2)
        silu_ffn(META, W_FFN1 + 8)
        silu_ffn(META, W_MIX + 8)
        assert not side
        dilated_mixer(W_FFN2 + 8, band_tok[0])
        silu_ffn(META, None)
        q.wait("sp", done[-1])
        assert len(spent) == len(order) and len(split) == len(order)

        sems = {s: ctx.enter_context(nc.semaphore(f"s_{s}")) for s in q.count}
        block = ctx.enter_context(nc.Block())

        @block.sync
        def _(eng):
            q.run("sp", eng, sems)

        @block.gpsimd
        def _(eng):
            q.run("pool", eng, sems)

        @block.scalar
        def _(eng):
            q.run("act", eng, sems)

        @block.vector
        def _(eng):
            q.run("dve", eng, sems)

        @block.tensor
        def _(eng):
            q.run("pe", eng, sems)


WEIGHTS = ["ffn1_w_gate", "ffn1_w_up", "ffn1_w_down", "w_in", "w_out", "ffn2_w_gate", "ffn2_w_up", "ffn2_w_down",
           "ffn1_w_in_2", "ffn1_w_out_2", "conv_w_in_2", "conv_w_out_2", "attn_w_qkv_2", "attn_w_out_2",
           "rel_bias_2", "ffn2_w_in_2", "ffn2_w_out_2"]


def kernel(**inputs):
    import concourse.bacc as bacc
    from concourse.bass_utils import run_bass_kernel_spmd

    a = {k: np.ascontiguousarray(v) for k, v in inputs.items()}

    def cols(v):
        return v.reshape(-1, KC, P).transpose(2, 0, 1).reshape(P, -1)

    vec = np.concatenate(
        [cols(a[n]) for n in ("ffn1_norm", "mix_norm", "ffn2_norm", "final_norm", "norm_ffn1_2", "norm_mix_2",
                              "norm_ffn2_2", "conv_w_2")]
        + [a["ret_gn_w"].reshape(8, P).T, a["diff_subln_w"].T]
        + [np.concatenate([a[n][0].T, a[n][0].T], axis=0) for n in ("attn_q_gain_2", "attn_k_gain_2")], axis=1)
    lam = np.concatenate([a[n] for n in ("diff_lambda_q1", "diff_lambda_q2", "diff_lambda_k1", "diff_lambda_k2")]).T
    arrays = {n: a[n] for n in WEIGHTS}
    arrays["hT"] = np.ascontiguousarray(np.concatenate([a["meta_tokens"], a["x"][0]]).T)
    arrays["vec"] = np.ascontiguousarray(vec)
    arrays["lam"] = np.ascontiguousarray(lam)
    arrays.update(constants())

    nc = bacc.Bacc("TRN2", target_bir_lowering=False, num_devices=1)
    aps = {n: nc.dram_tensor(n, v.shape, mybir.dt.from_np(v.dtype), kind="ExternalInput").ap()
           for n, v in arrays.items()}
    out = nc.dram_tensor("outT", (D, SEQ), F32, kind="ExternalOutput").ap()
    build(nc, aps, out)
    r = run_bass_kernel_spmd(nc, [arrays], core_ids=[0])
    return np.ascontiguousarray(r.results[0]["outT"].T).reshape(1, SEQ, D)
```
